# Optimizing a Trainium2 kernel written in Bass

```python
import math
import jax
import jax.numpy as jnp
from jax import lax
import numpy as np

D_MODEL = 1024
BATCH = 1
SEQ = 256
DEPTH = 1

CHUNK = 64
N_META = 16
N_HEADS = 8
HEAD_DIM = 64
V_DIM = 2 * HEAD_DIM
QK_W = N_HEADS * 2 * HEAD_DIM
ATTN_W = N_HEADS * V_DIM
Q_BLOCK = 128
CONV_C = D_MODEL
CONV_K = 31
N_EXPERTS = 32
TOP_K = 4
D_EXPERT = D_MODEL
SWIGLU_ALPHA = 1.702
SWIGLU_LIMIT = 7.0
EXPERT_BLOCK = 256
EPS = 1e-5
IN_W = 2 * QK_W + ATTN_W + 2 * CONV_C + 2 * D_MODEL
SPLITS = [QK_W, 2 * QK_W, 2 * QK_W + ATTN_W, 2 * QK_W + ATTN_W + CONV_C,
          2 * QK_W + ATTN_W + 2 * CONV_C, 2 * QK_W + ATTN_W + 2 * CONV_C + D_MODEL]

kernel_name = "hybrid_diffattn_conformer_conv_moe_stream"

def _rmsnorm(x, g):
    xf = x.astype(jnp.float32)
    y = xf * lax.rsqrt(jnp.mean(xf * xf, axis=-1, keepdims=True) + EPS)
    return (y * g.astype(jnp.float32)).astype(x.dtype)

def _layernorm(x, g, b):
    xf = x.astype(jnp.float32)
    mu = jnp.mean(xf, axis=-1, keepdims=True)
    var = jnp.mean(jnp.square(xf - mu), axis=-1, keepdims=True)
    y = (xf - mu) * lax.rsqrt(var + EPS)
    return (y * g.astype(jnp.float32) + b.astype(jnp.float32)).astype(x.dtype)

def _alibi_slopes():
    return jnp.asarray([2.0 ** (-8.0 * (h + 1) / N_HEADS) for h in range(N_HEADS)],
                       dtype=jnp.float32)

def _chunk_ids(length):
    pos = jnp.arange(length, dtype=jnp.int32)
    return jnp.where(pos < N_META, 0, (pos - N_META) // CHUNK + 1)

def _visible_end(i, length):
    if i < N_META:
        end = N_META
    else:
        end = N_META + ((i - N_META) // CHUNK + 1) * CHUNK
    return min(end, length)

def _diff_attention(q, k, v, lam):
    length = q.shape[3]
    pos = jnp.arange(length, dtype=jnp.int32)
    chunk = _chunk_ids(length)
    slopes = _alibi_slopes()
    scale = HEAD_DIM ** -0.5
    outs = []
    for s0 in range(0, length, Q_BLOCK):
        s1 = min(s0 + Q_BLOCK, length)
        kend = _visible_end(s1 - 1, length)
        s = jnp.einsum("bhmqd,bhmkd->bhmqk", q[:, :, :, s0:s1],
                       k[:, :, :, :kend]).astype(jnp.float32) * scale
        dist = jnp.abs(pos[s0:s1, None] - pos[None, :kend]).astype(jnp.float32)
        bias = -slopes[:, None, None] * dist
        visible = chunk[None, :kend] <= chunk[s0:s1, None]
        s = jnp.where(visible, s + bias[None, :, None], -jnp.inf)
        p = jax.nn.softmax(s, axis=-1)
        a = p[:, :, 0] - lam * p[:, :, 1]
        outs.append(jnp.einsum("bhqk,bhkd->bhqd", a.astype(v.dtype), v[:, :, :kend]))
    return jnp.concatenate(outs, axis=2)

def _conformer_conv(ca, cb, w_dw, b_dw, ln_g, ln_b, w_pw):
    u = ca * jax.nn.sigmoid(cb)
    y = lax.conv_general_dilated(u, w_dw[:, None, :].astype(u.dtype), (1,),
                                 [(CONV_K - 1, 0)],
                                 dimension_numbers=("NWC", "WIO", "NWC"),
                                 feature_group_count=CONV_C)
    y = jax.nn.silu(_layernorm(y + b_dw, ln_g, ln_b))
    return y @ w_pw

def _moe(h, w_router, b_router, w_gu, b_gu, w_dn, b_dn):
    n, d = h.shape
    logits = (h @ w_router + b_router).astype(jnp.float32)
    top_logit, top_idx = lax.top_k(logits, TOP_K)
    gates = jax.nn.softmax(top_logit, axis=-1)
    n_assign = n * TOP_K
    e_flat = top_idx.reshape(n_assign).astype(jnp.int32)
    tok_flat = jnp.arange(n_assign, dtype=jnp.int32) // TOP_K
    g_flat = gates.reshape(n_assign)
    order = jnp.argsort(e_flat)
    e_sorted = e_flat[order]
    counts = jnp.zeros((N_EXPERTS,), jnp.int32).at[e_flat].add(1)
    padded = (counts + EXPERT_BLOCK - 1) // EXPERT_BLOCK * EXPERT_BLOCK
    pad_end = jnp.cumsum(padded)
    pad_start = pad_end - padded
    grp_start = jnp.cumsum(counts) - counts
    dest = pad_start[e_sorted] + (jnp.arange(n_assign, dtype=jnp.int32) - grp_start[e_sorted])
    n_blocks = -(-(n_assign + N_EXPERTS * (EXPERT_BLOCK - 1)) // EXPERT_BLOCK)
    n_slots = n_blocks * EXPERT_BLOCK
    slot_tok = jnp.full((n_slots,), n, jnp.int32).at[dest].set(tok_flat[order])
    slot_gate = jnp.zeros((n_slots,), jnp.float32).at[dest].set(g_flat[order])
    block_start = jnp.arange(n_blocks, dtype=jnp.int32) * EXPERT_BLOCK
    block_exp = jnp.minimum(jnp.searchsorted(pad_end, block_start, side="right"),
                            N_EXPERTS - 1)
    h_pad = jnp.concatenate([h, jnp.zeros((1, d), h.dtype)], axis=0)

    def expert_block(args):
        tok, e = args
        xb = h_pad[tok]
        gu = xb @ w_gu[e] + b_gu[e]
        glu = jnp.minimum(gu[:, :D_EXPERT], SWIGLU_LIMIT)
        lin = jnp.clip(gu[:, D_EXPERT:], -SWIGLU_LIMIT, SWIGLU_LIMIT)
        act = glu * jax.nn.sigmoid(SWIGLU_ALPHA * glu) * (lin + 1.0)
        return act @ w_dn[e] + b_dn[e]

    ys = lax.map(expert_block, (slot_tok.reshape(n_blocks, EXPERT_BLOCK), block_exp))
    ys = ys.reshape(n_slots, d) * slot_gate[:, None].astype(h.dtype)
    return jnp.zeros((n + 1, d), h.dtype).at[slot_tok].add(ys)[:n]

def setup_inputs(seed: int = 0) -> dict:
    key = jax.random.key(seed)
    ks = jax.random.split(key, 24)

    def nrm(k, shape, s):
        return jax.random.normal(k, shape, jnp.float32) * s

    return {
        "x": nrm(ks[0], (BATCH, SEQ, D_MODEL), 1.0),
        "meta_tokens": nrm(ks[1], (N_META, D_MODEL), 1.0),
        "norm_mix": 1.0 + nrm(ks[2], (DEPTH, D_MODEL), 0.05),
        "w_in": nrm(ks[3], (DEPTH, D_MODEL, IN_W), D_MODEL ** -0.5),
        "b_in": nrm(ks[4], (DEPTH, IN_W), 0.02),
        "lam_params": nrm(ks[5], (DEPTH, 4, HEAD_DIM), 0.1),
        "subln_gain": 1.0 + nrm(ks[6], (DEPTH, V_DIM), 0.05),
        "w_attn_proj": nrm(ks[7], (DEPTH, ATTN_W, D_MODEL), ATTN_W ** -0.5),
        "conv_dw_w": nrm(ks[8], (DEPTH, CONV_K, CONV_C), CONV_K ** -0.5),
        "conv_dw_b": nrm(ks[9], (DEPTH, CONV_C), 0.02),
        "conv_ln_g": 1.0 + nrm(ks[10], (DEPTH, CONV_C), 0.05),
        "conv_ln_b": nrm(ks[11], (DEPTH, CONV_C), 0.02),
        "w_conv_proj": nrm(ks[12], (DEPTH, CONV_C, D_MODEL), CONV_C ** -0.5),
        "w_out": nrm(ks[13], (DEPTH, D_MODEL, D_MODEL), D_MODEL ** -0.5),
        "norm_ffn": 1.0 + nrm(ks[14], (DEPTH, D_MODEL), 0.05),
        "w_router": nrm(ks[15], (DEPTH, D_MODEL, N_EXPERTS), D_MODEL ** -0.5),
        "b_router": nrm(ks[16], (DEPTH, N_EXPERTS), 0.01),
        "w_gate_up": nrm(ks[17], (DEPTH, N_EXPERTS, D_MODEL, 2 * D_EXPERT), D_MODEL ** -0.5),
        "b_gate_up": nrm(ks[18], (DEPTH, N_EXPERTS, 2 * D_EXPERT), 0.02),
        "w_down": nrm(ks[19], (DEPTH, N_EXPERTS, D_EXPERT, D_MODEL), D_EXPERT ** -0.5),
        "b_down": nrm(ks[20], (DEPTH, N_EXPERTS, D_MODEL), 0.02),
        "norm_final": 1.0 + nrm(ks[21], (D_MODEL,), 0.05),
    }

def reference(x, meta_tokens, norm_mix, w_in, b_in, lam_params, subln_gain, w_attn_proj,
              conv_dw_w, conv_dw_b, conv_ln_g, conv_ln_b, w_conv_proj, w_out, norm_ffn,
              w_router, b_router, w_gate_up, b_gate_up, w_down, b_down, norm_final):
    bsz = x.shape[0]
    meta = jnp.broadcast_to(meta_tokens[None].astype(x.dtype), (bsz, N_META, D_MODEL))
    h = jnp.concatenate([meta, x], axis=1)
    length = h.shape[1]
    for layer in range(DEPTH):
        xn = _rmsnorm(h, norm_mix[layer])
        proj = xn @ w_in[layer] + b_in[layer]
        q, k, v, ca, cb, ga, gc = jnp.split(proj, SPLITS, axis=-1)
        q = q.reshape(bsz, length, N_HEADS, 2, HEAD_DIM).transpose(0, 2, 3, 1, 4)
        k = k.reshape(bsz, length, N_HEADS, 2, HEAD_DIM).transpose(0, 2, 3, 1, 4)
        v = v.reshape(bsz, length, N_HEADS, V_DIM).transpose(0, 2, 1, 3)
        lp = lam_params[layer].astype(jnp.float32)
        lam_init = 0.8 - 0.6 * math.exp(-0.3 * layer)
        lam = jnp.exp(jnp.sum(lp[0] * lp[1])) - jnp.exp(jnp.sum(lp[2] * lp[3])) + lam_init
        o = _diff_attention(q, k, v, lam)
        o = _rmsnorm(o, subln_gain[layer]) * (1.0 - lam_init)
        o = o.transpose(0, 2, 1, 3).reshape(bsz, length, ATTN_W)
        y_attn = o @ w_attn_proj[layer]
        y_conv = _conformer_conv(ca, cb, conv_dw_w[layer], conv_dw_b[layer],
                                 conv_ln_g[layer], conv_ln_b[layer], w_conv_proj[layer])
        mixed = jax.nn.sigmoid(ga) * y_attn + jax.nn.sigmoid(gc) * y_conv
        h = h + mixed @ w_out[layer]
        hn = _rmsnorm(h, norm_ffn[layer]).reshape(bsz * length, D_MODEL)
        moe = _moe(hn, w_router[layer], b_router[layer], w_gate_up[layer],
                   b_gate_up[layer], w_down[layer], b_down[layer])
        h = h + moe.reshape(bsz, length, D_MODEL)
    return _rmsnorm(h, norm_final)[:, N_META:]


_drawn_inputs = setup_inputs


def setup_inputs(seed=0):
    import zlib

    import numpy as np

    out = dict(_drawn_inputs(seed))
    spreads = {}
    factors = {'conv_ln_b': 3.193, 'b_gate_up': 5.672, 'b_down': 6.493}
    for name, (base, spread) in spreads.items():
        noise = np.random.default_rng([zlib.crc32(name.encode()), seed]).standard_normal(out[name].shape)
        drawn = base * np.exp(spread * noise) if base else spread * noise
        out[name] = jnp.asarray(drawn.astype(out[name].dtype))
    for name, factor in factors.items():
        out[name] = (out[name] * factor).astype(out[name].dtype)
    return out
```

```python
import math
from contextlib import ExitStack

import concourse.bass as bass
from concourse import mybir

P = 128
BF16 = mybir.dt.bfloat16
F32 = mybir.dt.float32
I32 = mybir.dt.int32
U32 = mybir.dt.uint32
ALU = mybir.AluOpType
ACT = mybir.ActivationFunctionType
AX_X = mybir.AxisListType.X

CHUNK = 64
TOP_K = 4
ALPHA = 1.702
LIMIT = 7.0
EPS = 1e-5
LAM_INIT = 0.8 - 0.6 * math.exp(-0.3 * 0)
FAR = 1e30
RING = 6
WIDE = 4096


def encoder_block(nc, x, meta, norm_mix, w_in, b_in, lam_params, subln, w_attn, dw_w, dw_b,
                  ln_g, ln_b, w_conv, w_out, norm_ffn, w_router, b_router, w_gu, b_gu,
                  w_dn, b_dn, norm_final, out):
    D = x.shape[2]
    T = x.shape[1]
    M = meta.shape[0]
    L = M + T
    KC = D // P
    TT = T // P
    NH = D // P
    HD = 64
    E = w_router.shape[2]
    TAPS = dw_w.shape[1]
    PAD = TAPS - 1 - M
    SLOT = 64
    FH = D // 2
    SCALE = HD ** -0.5
    IN_SLOTS = w_in.shape[2] // 512
    assert (D, T, M, E, TAPS) == (1024, 256, 16, 32, 31)

    Q, K_, V, CA, CB, GA, GC = range(7)
    ORDER = [(CA, 0), (CB, 0), (CA, 1), (CB, 1), (GA, 0), (GC, 0), (GA, 1), (GC, 1),
             (Q, 0), (K_, 0), (V, 0), (Q, 1), (K_, 1), (V, 1)]
    assert len(ORDER) == IN_SLOTS
    TRUNK = IN_SLOTS + 6
    PER_EXPERT = 6

    assert RING == PER_EXPERT

    def moe_slot(j):
        return (TRUNK + j) % RING

    R_BIN, R_MIX = 0, w_in.shape[2] // P
    R_DWB = R_MIX + KC
    R_LNG = R_DWB + KC
    R_LNB = R_LNG + KC
    R_SUB = R_LNB + KC
    ROWS = R_SUB + 1

    with ExitStack() as ctx:
        def sb(name, shape, dt=F32):
            return ctx.enter_context(nc.sbuf_tensor(name, shape, dt))

        def sem(name):
            return ctx.enter_context(nc.semaphore(name))

        bank = [ctx.enter_context(nc.psum_tensor(f"bank{i}", [P, 512], F32)) for i in range(4)]
        score_ps = ctx.enter_context(nc.psum_tensor("score_ps", [P, 2, 512], F32))
        bank += [score_ps[:, 0, :], score_ps[:, 1, :]]
        bank += [ctx.enter_context(nc.psum_tensor(f"bank{i}", [P, 512], F32)) for i in (6, 7)]

        ring = sb("ring", [P, RING, WIDE])
        h = sb("h", [P, TT, D])
        h_meta = sb("h_meta", [P, D])
        h_norm = sb("h_norm", [P, 3, D])
        xT = sb("xT", [P, KC, L])
        qT = sb("qT", [P, NH, T])
        kT = sb("kT", [P, NH, L])
        vT = sb("vT", [P, NH, L])
        u = sb("u", [P, KC, PAD + L])
        cbT = sb("cbT", [P, KC, L])
        gaT = sb("gaT", [P, KC, T])
        gcT = sb("gcT", [P, KC, T])
        SW = M + P + L
        dist = sb("dist", [P, SW])
        s_sb = sb("s_sb", [P, 2, 2, SW])
        a_sb = sb("a_sb", [P, SW])
        aT = sb("aT", [P, 5, P])
        o_sb = sb("o_sb", [P, 2, 2, P])
        junk = sb("junk", [P, 2, P])
        att = sb("att", [P, 2, 32])
        ident = sb("ident", [P, P])
        eye3 = sb("eye3", [P, E + 1], BF16)
        ones = sb("ones", [P, P])
        before = sb("before", [P, P])
        iota2 = sb("iota2", [P, 2, SLOT])
        thr = sb("thr", [P, 3])
        early = s_sb[:, :, :, :].rearrange("p a m c -> p (a m c)")
        rows = early[:, 0:P]
        dw_rows = early[:, P:3 * P].rearrange("p (a c) -> p a c", a=2)
        lam_in = early[:, 3 * P:5 * P].rearrange("p (a c) -> p a c", a=4)
        cols = sb("cols", [P, ROWS])
        taps = sb("taps", [P, TAPS * KC])
        wr = sb("wr", [P, KC, E])
        br = sb("br", [P, E])
        st = sb("st", [P, 32])
        rt = sb("rt", [P, 2, 32])
        flag = sb("flag", [P, 1], I32)

        v_tok = h_norm[:, :, :].rearrange("p b (h d) -> p b h d", d=P)
        oT = vT[:, :, 0:T]
        yT = cbT[:, :, 0:T]
        gain_ffn = cbT[:, :, :].rearrange("p c t -> p (c t)")[:, 0:D]
        gain_fin = h_norm[:, 0, :]
        fin = h_norm[:, 1:3, :]
        hn = qT[:, :, :].rearrange("p c t -> p (c t)").rearrange("p (a d) -> p a d", a=TT)
        kflat = kT[:, :, :].rearrange("p c t -> p (c t)")
        glu_c, lin_c, sig, act = [kflat[:, i * FH:(i + 1) * FH] for i in range(4)]
        uflat = u[:, :, :].rearrange("p c t -> p (c t)")
        xg = [uflat[:, i * 512:(i + 1) * 512].rearrange("p (c s) -> p c s", s=SLOT) for i in range(2)]
        actT = uflat[:, 1024:1536].rearrange("p (b z s) -> p b z s", z=2, s=SLOT)
        y_sb = uflat[:, 1536:2048]
        xflat = xT[:, :, :].rearrange("p c t -> p (c t)")
        scat = [xflat[:, i * T:(i + 1) * T] for i in range(2)]
        pick = xflat[:, 512:576].bitcast(BF16).rearrange("p (a s) -> p a s", a=TT)
        gpick = xflat[:, 640:896].rearrange("p (a z s) -> p a z s", a=TT, z=2)
        esel = [xflat[0:3 * E, 896 + i * 32:928 + i * 32].bitcast(BF16) for i in range(2)]
        GP = E + 1
        gate = xflat[:, 1024:1024 + TT * GP].rearrange("p (a e) -> p a e", a=TT)
        slot = xflat[:, 1100:1100 + TT * GP].rearrange("p (a e) -> p a e", a=TT)
        member = xflat[:, 1168:1168 + TT * E].rearrange("p (a e) -> p a e", a=TT)
        eqs = xflat[:, 1232:1232 + TT * 4 * E].rearrange("p (a j e) -> p a j e", a=TT, j=4)
        logits = xflat[:, 1488:1488 + TT * E].rearrange("p (a e) -> p a e", a=TT)
        gateT = xflat[:, 1552:1552 + T]
        counts = xflat[:, 1808:1808 + E]
        top8 = xflat[:, 1840:1856].rearrange("p (a k) -> p a k", a=TT)
        idx8 = xflat[:, 1856:1872].bitcast(U32).rearrange("p (a k) -> p a k", a=TT)
        idxf = xflat[:, 1872:1888].rearrange("p (a k) -> p a k", a=TT)
        bias_gu = h_meta[0:3 * E, :].bitcast(BF16)
        bias_f32 = uflat[0:3 * E, 0:2 * D]
        hn_parts = [gaT[:, 0:4, :], gaT[:, 4:8, :], gcT[:, 0:4, :]]
        hn_parts = [a.rearrange("p c t -> p (c t)").bitcast(BF16).rearrange("p (a d) -> p a d", a=TT) for a in hn_parts]
        hnT = kflat[:, 0:2048].rearrange("p (a c t) -> p a c t", a=TT, c=KC)
        bias_dn = vT[:, :, :].rearrange("p c t -> p (c t)")[:, 0:D]

        loaded = [sem(f"loaded{s}") for s in range(RING)]
        freed = [sem(f"freed{s}") for s in range(RING)]
        x_in = [sem(f"x_in{t}") for t in range(3)]
        vec_in, lam_ld, small_in, taps_in = sem("vec_in"), sem("lam_ld"), sem("small_in"), sem("taps_in")
        gain_in, gainf_in, bdn_in, bgu_in = sem("gain_in"), sem("gainf_in"), sem("bdn_in"), sem("bgu_in")
        const_ok = sem("const_ok")
        sq_ok, rs_ok, var_ok, hs_ok = sem("sq_ok"), sem("rs_ok"), sem("var_ok"), sem("hs_ok")
        vec_ps, vec_ok = sem("vec_ps"), sem("vec_ok")
        xT_ps, xT_ok = sem("xT_ps"), sem("xT_ok")
        proj_ps, proj_ok = sem("proj_ps"), sem("proj_ok")
        dve = sem("dve")
        pool = sem("pool")
        u_ok, conv_ok = sem("u_ok"), sem("conv_ok")
        mean_ps, cen_ok, csq_ok, csq_used, cvar_ps = [sem(n) for n in ("mean_ps", "cen_ok", "csq_ok", "csq_used", "cvar_ps")]
        cvar_ok, cstd_ok, z_ok, y_ok = [sem(n) for n in ("cvar_ok", "cstd_ok", "z_ok", "y_ok")]
        lam_arg, lam_exp = sem("lam_arg"), sem("lam_exp")
        score_done, score_read, negmax_ok, exp_ok = [sem(n) for n in ("score_done", "score_read", "negmax_ok", "exp_ok")]
        a_ok, t_ps, t_ok = sem("a_ok"), sem("t_ps"), sem("t_ok")
        m_ps, m_ok = sem("m_ps"), sem("m_ok")
        osq_ok, ovar_ok, ostd_ok, on_ok = [sem(n) for n in ("osq_ok", "ovar_ok", "ostd_ok", "on_ok")]
        mix_ps, mix_ok, mixed_ok = sem("mix_ps"), sem("mix_ok"), sem("mixed_ok")
        out_ps, h_ok, hsq_ok, hvar_ok, hstd_ok, hn_ok = [sem(n) for n in ("out_ps", "h_ok", "hsq_ok", "hvar_ok", "hstd_ok", "hn_ok")]
        hT_ps, hT_ok, lg_ps, topn_ok, tope_ok, memb_ok = [sem(n) for n in ("hT_ps", "hT_ok", "lg_ps", "topn_ok", "tope_ok", "memb_ok")]
        num_ps, gT_ps, gT_ok, acc_init, rounds_ok, zero_ok = [sem(n) for n in ("num_ps", "gT_ps", "gT_ok", "acc_init", "rounds_ok", "zero_ok")]
        pick_ok, gather_ps, xg_ok, scatT_ps, scatT_ok = [sem(n) for n in ("pick_ok", "gather_ps", "xg_ok", "scatT_ps", "scatT_ok")]
        part0_ok, part1_ok, part2_ok = sem("part0_ok"), sem("part1_ok"), sem("part2_ok")
        gu_read, sig_in, sig_ok, lin_ok, act_ok, shift_ok = [sem(n) for n in ("gu_read", "sig_in", "sig_ok", "lin_ok", "act_ok", "shift_ok")]
        actT_ps, actT_ok, ysb_ok, scat_done = [sem(n) for n in ("actT_ps", "actT_ok", "ysb_ok", "scat_done")]
        h2_ok, fsq_ok, fvar_ok, fstd_ok, frec_ok, fin_ok, stored = [sem(n) for n in (
            "h2_ok", "fsq_ok", "fvar_ok", "fstd_ok", "frec_ok", "fin_ok", "stored")]

        block = ctx.enter_context(nc.Block())

        TICKS = NH + 2
        LATE0 = 11 * 4
        late = [("in", c) for c in range(LATE0, IN_SLOTS * 4)] + [("conv", n) for n in range(KC)]
        tick_chunks = []
        for t in range(TICKS):
            n = 3 if t < 4 else 2 if t < 8 else 0
            piece, late = late[:n], late[n:]
            tick_chunks.append([piece[i] if i < len(piece) else None for i in range(3)])
        assert not late

        def run_chunk(kind, n):
            return ORDER.index((kind, n // 4)) * 4 + n % 4

        def uses(s):
            return len(range(s, TRUNK, RING))

        def trunk_through(n):
            return (proj_ps, 4 * (n + 1)) if n < TRUNK - 2 else (out_ps, 2 * TT)

        def gu_done(n):
            return freed[moe_slot(3)], n + 1

        def y_done(n):
            return freed[moe_slot(5)], n + 1

        m_seq = []
        for t in range(TICKS):
            m_seq += [("v", t)] * (t < NH) + [("o", t - 1)] * (0 <= t - 1 < NH) + [("n", t - 2)] * (t >= 2)
        m_no = {key: i for i, key in enumerate(m_seq)}

        @block.sync
        def _(sp):
            for t in range(TT):
                sp.dma_start(h[:, t, :], x[0, t * P:(t + 1) * P, :]).then_inc(x_in[t], 16)

            def group(w, c0):
                return w[0, :, c0:c0 + 512].rearrange("(k p) n -> p k n", p=P)

            sources = [group(w_in, (kind * 2 + half) * 512) for kind, half in ORDER]
            sources += [group(w_conv, 0), group(w_conv, 512), group(w_attn, 0), group(w_attn, 512)]
            sources += [w_out[0, a * FH:(a + 1) * FH, :].rearrange("(k p) n -> p k n", p=P) for a in range(2)]
            sp.wait_ge(x_in[2], 16)
            sp.wait_ge(vec_in, 16 * 6)
            sp.wait_ge(taps_in, 32)
            for n, src in enumerate(sources):
                if n >= RING:
                    sp.wait_ge(*trunk_through(n - RING))
                dst = ring[:, n % RING, :].rearrange("p (k n) -> p k n", k=src.shape[1])
                sp.dma_start(dst, src).then_inc(loaded[n % RING], 16)

            def load_expert(n, e):
                for j in range(PER_EXPERT):
                    s = moe_slot(j)
                    if isinstance(n, int) and n == 0:
                        sp.wait_ge(*trunk_through(TRUNK - RING + j))
                    else:
                        sp.wait_ge(freed[s], n)
                    if j < 4:
                        src = w_gu[0, bass.ds(e, 1), j * 256:(j + 1) * 256, :]
                        kk = 2
                    else:
                        src = w_dn[0, bass.ds(e, 1), (j - 4) * 512:(j - 3) * 512, :]
                        kk = 4
                    sp.dma_start(ring[:, s, :].rearrange("p (k n) -> p k n", k=kk),
                                 src.rearrange("a (k p) n -> p (a k) n", p=P)).then_inc(loaded[s], 16)

            load_expert(0, 0)
            with sp.Fori(1, E) as e:
                load_expert(e, e)
            sp.wait_ge(rounds_ok, 1)
            n_rounds = sp.value_load(flag[0:1, 0:1], min_val=1, max_val=T // SLOT)
            with sp.If(n_rounds > 1):
                with sp.Fori(1, n_rounds) as r:
                    with sp.Fori(0, E) as e:
                        load_expert(r * E + e, e)
            with sp.Else():
                sp.nop()
            for t in range(TT):
                sp.wait_ge(fin_ok, t + 1)
                sp.dma_start(out[0, t * P:(t + 1) * P, :], fin[:, t, :]).then_inc(stored, 16)
            sp.wait_ge(stored, 16 * TT)

        @block.gpsimd
        def _(gp):
            nc.gpsimd.memset(ident[:], 0.0).then_inc(pool, 1)
            nc.gpsimd.memset(ones[:], 1.0).then_inc(pool, 1)
            nc.gpsimd.memset(eye3[:], 0.0).then_inc(pool, 1)
            gp.wait_ge(pool, 3)
            nc.gpsimd.affine_select(out=ident[:], in_=ident[:], compare_op=ALU.not_equal, fill=1.0, base=0,
                                    pattern=[[-1, P]], channel_multiplier=1).then_inc(const_ok, 1)
            nc.gpsimd.affine_select(out=before[:], in_=ones[:], compare_op=ALU.is_gt, fill=0.0, base=0,
                                    pattern=[[1, P]], channel_multiplier=-1).then_inc(const_ok, 1)
            nc.gpsimd.iota(iota2[:], [[0, 2], [1, SLOT]], base=0, channel_multiplier=0,
                           allow_small_or_imprecise_dtypes=True).then_inc(const_ok, 1)
            nc.gpsimd.iota(thr[:], [[SLOT, 3]], base=SLOT, channel_multiplier=0,
                           allow_small_or_imprecise_dtypes=True).then_inc(const_ok, 1)
            nc.gpsimd.iota(dist[:, 0:M + P], [[-1, M + P]], base=M, channel_multiplier=1,
                           allow_small_or_imprecise_dtypes=True).then_inc(const_ok, 1)
            nc.gpsimd.iota(dist[:, M + P:SW], [[-1, L]], base=M + P, channel_multiplier=1,
                           allow_small_or_imprecise_dtypes=True).then_inc(const_ok, 1)
            for j in range(3):
                if j:
                    gp.wait_ge(pool, 3 + j)
                nc.gpsimd.affine_select(out=eye3[:], in_=eye3[:], compare_op=ALU.not_equal, fill=1.0, base=-E * j,
                                        pattern=[[-1, E + 1]], channel_multiplier=1).then_inc(pool, 1)
            gp.wait_ge(conv_ok, KC)
            for j in range(3):
                gp.dma_start(bias_f32[j * E:(j + 1) * E, :], b_gu[0]).then_inc(bgu_in, 16)
            gp.wait_ge(bgu_in, 48)
            nc.gpsimd.tensor_copy(bias_gu, bias_f32).then_inc(pool, 1)
            gp.wait_ge(pool, 7)
            for j in (1, 2):
                for q in range(j, 3):
                    r = slice(q * E, (q + 1) * E)
                    nc.gpsimd.tensor_tensor(bias_f32[r, :], bias_f32[r, :], bias_gu[r, :], ALU.subtract).then_inc(pool, 1)
                gp.wait_ge(pool, 9 if j == 1 else 12)
                for q in range(j, 3):
                    r = slice(q * E, (q + 1) * E)
                    nc.gpsimd.tensor_copy(bias_gu[r, :], bias_f32[r, :]).then_inc(pool, 1)
                gp.wait_ge(pool, 11 if j == 1 else 13)
            gp.wait_ge(proj_ps, IN_SLOTS * 4 + KC)
            gp.dma_start(gain_ffn, norm_ffn[0].partition_broadcast(P)).then_inc(gain_in, 16)
            gp.wait_ge(mixed_ok, KC)
            gp.dma_start(bias_dn[0:E, :], b_dn[0]).then_inc(bdn_in, 16)
            gp.dma_start(gain_fin, norm_final.partition_broadcast(P)).then_inc(gainf_in, 16)
            for t in range(TT):
                gp.wait_ge(part1_ok, t + 1)
                nc.gpsimd.tensor_tensor(hn_parts[2][:, t, :], hn[:, t, :], hn_parts[1][:, t, :],
                                        ALU.subtract).then_inc(part2_ok, 1)

        CONSTS = 6

        @block.scalar
        def _(act_e):
            A = nc.scalar.activation
            act_e.dma_start(h_meta[0:M, :], meta).then_inc(x_in[2], 16)
            for r0, src in ((R_BIN, b_in), (R_MIX, norm_mix), (R_DWB, dw_b), (R_LNG, ln_g), (R_LNB, ln_b), (R_SUB, subln)):
                n = src.shape[1] // P
                act_e.dma_start(rows[r0:r0 + n, :], src.rearrange("a (r p) -> (a r) p", p=P)).then_inc(vec_in, 16)
            half = TAPS * KC // 2
            taps_rows = dw_w[0].rearrange("k (c p) -> (k c) p", p=P)
            for a in range(2):
                act_e.dma_start(dw_rows[0:half, a, :], taps_rows[a * half:(a + 1) * half, :]).then_inc(taps_in, 16)
            act_e.dma_start(lam_in, lam_params[0].partition_broadcast(P)).then_inc(lam_ld, 16)
            act_e.dma_start(wr[:], w_router[0].rearrange("(c p) e -> p c e", p=P)).then_inc(small_in, 16)
            act_e.dma_start(br[:], b_router[0].partition_broadcast(P)).then_inc(small_in, 16)

            act_e.wait_ge(lam_arg, 1)
            A(st[:, 8:10], st[:, 6:8], ACT.Exp).then_inc(lam_exp, 1)
            act_e.wait_ge(zero_ok, 1)
            for t in range(3):
                act_e.wait_ge(x_in[t], 16)
                src = h[:, t, :] if t < 2 else h_meta[0:M, :]
                n = P if t < 2 else M
                A(h_norm[0:n, t, :], src, ACT.Square, accum_out=st[0:n, t:t + 1]).then_inc(sq_ok, 1)
            act_e.wait_ge(var_ok, 1)
            A(st[:, 3:6], st[:, 0:3], ACT.Sqrt).then_inc(rs_ok, 1)

            def evacuate(c):
                kind, hf = ORDER[c // 4]
                n = hf * 4 + c % 4
                dst = {Q: qT[:, n, :], K_: kT[:, n, :], V: vT[:, n, :], CA: u[:, n, PAD:PAD + L],
                       CB: cbT[:, n, :], GA: gaT[:, n, :], GC: gcT[:, n, :]}[kind]
                fn = ACT.Sigmoid if kind in (CB, GA, GC) else ACT.Identity
                width = T if kind in (Q, GA, GC) else L
                col = R_BIN + kind * KC + n
                act_e.wait_ge(proj_ps, c + 1)
                A(dst, bank[c % 4][:, 0:width], fn, bias=cols[:, col:col + 1]).then_inc(proj_ok, 1)

            act_e.wait_ge(vec_ok, 1)
            for c in range(9 * 4):
                evacuate(c)
            for j in range(4):
                for c in (2 * j, 2 * j + 1):
                    act_e.wait_ge(cen_ok, c + 1)
                    if c >= 2:
                        act_e.wait_ge(csq_used, c - 1)
                    A(s_sb[:, 0, c % 2, 0:T], yT[:, c, :], ACT.Square).then_inc(csq_ok, 1)
                evacuate(9 * 4 + j)
            evacuate(10 * 4)
            act_e.wait_ge(cvar_ok, 1)
            A(s_sb[:, 1, 0, 0:T], s_sb[:, 1, 0, 0:T], ACT.Sqrt).then_inc(cstd_ok, 1)
            for j in range(1, 4):
                evacuate(10 * 4 + j)
            for c in range(KC):
                act_e.wait_ge(z_ok, c + 1)
                A(yT[:, c, :], yT[:, c, :], ACT.Silu, scale=cols[:, R_LNG + c:R_LNG + c + 1],
                  bias=cols[:, R_LNB + c:R_LNB + c + 1]).then_inc(y_ok, 1)

            for t in range(TICKS):
                g = t - 1
                if t < NH:
                    p = t % 2
                    act_e.wait_ge(negmax_ok, t + 1)
                    for m in range(2):
                        for qt, (c0, c1) in enumerate(((0, M + P), (M + P, SW))):
                            z = 8 + 2 * qt + m
                            A(s_sb[:, p, m, c0:c1], s_sb[:, p, m, c0:c1], ACT.Exp, scale=SCALE,
                              bias=att[:, p, 4 + 2 * qt + m:5 + 2 * qt + m],
                              accum_out=att[:, p, z:z + 1]).then_inc(exp_ok, 1)
                for i, piece in enumerate(tick_chunks[t]):
                    if piece and piece[0] == "in":
                        evacuate(piece[1])
                    if 0 <= g < NH and i < 2:
                        act_e.wait_ge(t_ps, 2 * g + i + 1)
                        if g >= 1:
                            act_e.wait_ge(m_ps, m_no["o", g - 1] + 1)
                        nb = 2 - i
                        b0 = 3 * i
                        nc.scalar.copy(aT[:, b0:b0 + nb, :], bank[6][:, 0:nb * P].rearrange("p (b q) -> p b q", q=P))
                        nc.scalar.copy(aT[0:M, b0 + nb, :], bank[6][0:M, nb * P:(nb + 1) * P]).then_inc(t_ok, 1)
                if 0 <= g < NH:
                    p = g % 2
                    act_e.wait_ge(m_ok, m_no["o", g] + 1)
                    for qt in range(2):
                        A(junk[:, qt, :], o_sb[:, p, qt, :], ACT.Square, accum_out=att[:, p, 16 + qt:17 + qt]).then_inc(osq_ok, 1)
                    act_e.wait_ge(ovar_ok, g + 1)
                    A(att[:, p, 20:22], att[:, p, 18:20], ACT.Sqrt).then_inc(ostd_ok, 1)

            for t in range(TT):
                act_e.wait_ge(h_ok, 2 * (t + 1))
                A(hn[:, t, :], h[:, t, :], ACT.Square, accum_out=st[:, 12 + t:13 + t]).then_inc(hsq_ok, 1)
                act_e.wait_ge(hvar_ok, t + 1)
                A(st[:, 14 + t:15 + t], st[:, 12 + t:13 + t], ACT.Sqrt).then_inc(hstd_ok, 1)
            for t in range(TT):
                act_e.wait_ge(out_ps, 2 * TT)
                act_e.wait_ge(hn_ok, t + 1)
                nc.scalar.copy(hn_parts[0][:, t, :], hn[:, t, :]).then_inc(part0_ok, 1)
            for t in range(TT):
                act_e.wait_ge(topn_ok, t + 1)
                A(rt[:, t, 4:8], top8[:, t, 0:TOP_K], ACT.Exp, bias=rt[:, t, 0:1],
                  accum_out=rt[:, t, 8:9]).then_inc(tope_ok, 1)

            def prepared(k, par):
                act_e.wait_ge(gather_ps, k + 1)
                nc.scalar.copy(xg[par], bank[6][:, :].rearrange("p (c s) -> p c s", s=SLOT)).then_inc(xg_ok, 1)
                act_e.wait_ge(scatT_ps, k + 1)
                nc.scalar.copy(scat[par], bank[7][:, 0:T]).then_inc(scatT_ok, 1)

            def expert(n, k, par):
                prepared(k, 1 - par)
                act_e.wait_ge(sig_in, n + 1)
                A(sig, glu_c, ACT.Sigmoid, scale=ALPHA).then_inc(sig_ok, 1)
                act_e.wait_ge(actT_ps, n + 1)
                nc.scalar.copy(actT, bank[7][:, :].rearrange("p (b z s) -> p b z s", z=2, s=SLOT)).then_inc(actT_ok, 1)
                act_e.wait_ge(*y_done(n))
                act_e.wait_ge(scat_done, n + 1)
                nc.scalar.copy(y_sb, bank[6][:, :]).then_inc(ysb_ok, 1)

            prepared(0, 0)
            with act_e.Fori(0, E // 2) as i:
                for par in range(2):
                    expert(i * 2 + par, i * 2 + (par + 1), par)
            act_e.wait_ge(rounds_ok, 1)
            n_rounds = act_e.value_load(flag[0:1, 0:1], min_val=1, max_val=T // SLOT)
            with act_e.If(n_rounds > 1):
                with act_e.Fori(1, n_rounds) as r:
                    prepared(r * GP, 0)
                    with act_e.Fori(0, E // 2) as i:
                        for par in range(2):
                            expert(r * E + i * 2 + par, r * GP + i * 2 + (par + 1), par)
            with act_e.Else():
                act_e.nop()
            for t in range(TT):
                act_e.wait_ge(h2_ok, 2 * (t + 1))
                A(fin[:, t, :], h[:, t, :], ACT.Square, accum_out=st[:, 20 + t:21 + t]).then_inc(fsq_ok, 1)
            act_e.wait_ge(fvar_ok, 1)
            A(st[:, 22:24], st[:, 20:22], ACT.Sqrt).then_inc(fstd_ok, 1)

        @block.vector
        def _(ve):
            dv = nc.vector
            made = [0]

            def step(ins):
                ins.then_inc(dve, 1)
                made[0] += 1

            def settle(behind=0):
                ve.wait_ge(dve, made[0] - behind)

            dv.memset(st[:], 0.0).then_inc(zero_ok, 1)
            dv.memset(u[:, :, 0:PAD], 0.0)
            ve.wait_ge(const_ok, CONSTS)
            step(dv.scalar_tensor_tensor(dist[:], dist[:], -1.0, dist[:], ALU.mult, ALU.max))
            settle()
            step(dv.memset(dist[0:CHUNK, M + CHUNK:M + P], FAR))
            step(dv.memset(dist[0:CHUNK, SW - CHUNK:SW], FAR))

            ve.wait_ge(vec_ps, 1)
            dv.tensor_copy(cols[:], bank[7][:, 0:ROWS])
            dv.tensor_copy(taps[:], bank[7][:, P:P + TAPS * KC]).then_inc(vec_ok, 1)

            ve.wait_ge(lam_ld, 16)
            prod = junk[:, :, 0:HD]
            step(dv.tensor_tensor(prod, lam_in[:, 0:4:2, :], lam_in[:, 1:4:2, :], ALU.mult))
            settle()
            dv.reduce_sum(st[:, 6:8], prod, AX_X).then_inc(lam_arg, 1)
            ve.wait_ge(lam_exp, 1)
            step(dv.tensor_tensor(st[:, 10:11], st[:, 9:10], st[:, 8:9], ALU.subtract))
            settle()
            step(dv.tensor_scalar(st[:, 11:12], st[:, 10:11], -LAM_INIT, None, ALU.add))

            ve.wait_ge(sq_ok, 3)
            dv.tensor_scalar(st[:, 0:3], st[:, 0:3], 1.0 / D, EPS, ALU.mult, ALU.add).then_inc(var_ok, 1)
            ve.wait_ge(rs_ok, 1)
            step(dv.reciprocal(st[:, 3:6], st[:, 3:6]))
            settle()
            for t in range(3):
                n = P if t < 2 else M
                src = h[:, t, :] if t < 2 else h_meta[0:M, :]
                dv.tensor_scalar(h_norm[0:n, t, :], src, st[0:n, 3 + t:4 + t], None, ALU.mult).then_inc(hs_ok, 1)
            for c in range(KC):
                ve.wait_ge(xT_ps, c + 1)
                dv.tensor_scalar(xT[:, c, :], bank[c][:, 0:L], cols[:, R_MIX + c:R_MIX + c + 1], None,
                                ALU.mult).then_inc(xT_ok, 1)

            for c0 in range(0, KC, 2):
                pair = (c0, c0 + 1)
                for c in pair:
                    ve.wait_ge(proj_ok, (c // 4) * 8 + 4 + c % 4 + 1)
                    step(dv.tensor_tensor(u[:, c, PAD:PAD + L], u[:, c, PAD:PAD + L], cbT[:, c, :], ALU.mult))
                for c in pair:
                    settle(1)
                    step(dv.tensor_scalar(yT[:, c, :], u[:, c, 0:T], taps[:, c:c + 1],
                                         cols[:, R_DWB + c:R_DWB + c + 1], ALU.mult, ALU.add))
                for k in range(1, TAPS):
                    for c in pair:
                        settle(1)
                        step(dv.scalar_tensor_tensor(yT[:, c, :], u[:, c, k:k + T],
                                                    taps[:, k * KC + c:k * KC + c + 1], yT[:, c, :],
                                                    ALU.mult, ALU.add))
                settle()
                dv.tensor_copy(att[:, 0, 0:1], st[:, 0:1]).then_inc(conv_ok, 2)
            mean, std = s_sb[:, 1, 1, 0:T], s_sb[:, 1, 0, 0:T]
            ve.wait_ge(mean_ps, 1)
            step(dv.tensor_scalar(mean, bank[6][:, 0:T], 1.0 / D, None, ALU.mult))
            settle()
            for c in range(KC):
                dv.tensor_tensor(yT[:, c, :], yT[:, c, :], mean, ALU.subtract).then_inc(cen_ok, 1)
            ve.wait_ge(cvar_ps, 1)
            dv.tensor_scalar(std, bank[7][:, 0:T], 1.0 / D, EPS, ALU.mult, ALU.add).then_inc(cvar_ok, 1)
            ve.wait_ge(cstd_ok, 1)
            step(dv.reciprocal(std, std))
            settle()
            for c in range(KC):
                dv.tensor_tensor(yT[:, c, :], yT[:, c, :], std, ALU.mult).then_inc(z_ok, 1)

            def mix_conv(piece):
                n = piece[1]
                ve.wait_ge(proj_ps, IN_SLOTS * 4 + n + 1)
                dv.tensor_tensor(gcT[:, n, :], gcT[:, n, :], bank[n % 4][:, 0:T], ALU.mult).then_inc(mix_ok, 1)

            spans = ((0, M + P), (M + P, SW))
            for t in range(TICKS):
                g, f = t - 1, t - 2
                pieces = [p if p and p[0] == "conv" else None for p in tick_chunks[t]]
                if t < NH:
                    p = t % 2
                    slope = 2.0 ** (-8.0 * (t + 1) / NH)
                    ve.wait_ge(score_done, t + 1)
                    dv.scalar_tensor_tensor(s_sb[:, p, :, :], dist[:].unsqueeze(1).broadcast_to([P, 2, SW]),
                                           -slope / SCALE, score_ps[:, :, 0:SW], ALU.mult, ALU.add).then_inc(score_read, 1)
                    ve.wait_ge(score_read, t + 1)
                    for qt, (c0, c1) in enumerate(spans):
                        step(dv.reduce_max(att[:, p, 2 * qt:2 * qt + 2], s_sb[:, p, :, c0:c1], AX_X))
                    settle()
                    dv.tensor_scalar(att[:, p, 4:8], att[:, p, 0:4], -SCALE, None, ALU.mult).then_inc(negmax_ok, 1)
                    ve.wait_ge(m_ps, m_no["v", t] + 1)
                    dv.tensor_copy(v_tok[:, 0:2, t, :], bank[7][:, 0:2 * P].rearrange("p (b d) -> p b d", d=P))
                    dv.tensor_copy(v_tok[0:M, 2, t, :], bank[7][0:M, 2 * P:3 * P]).then_inc(m_ok, 1)
                for piece in pieces[0:2]:
                    if piece:
                        mix_conv(piece)
                if t < NH:
                    ve.wait_ge(exp_ok, 4 * (t + 1))
                    step(dv.reciprocal(att[:, p, 12:16], att[:, p, 8:12]))
                    settle()
                    step(dv.tensor_scalar(att[:, p, 13:16:2], att[:, p, 13:16:2], st[:, 11:12], None, ALU.mult))
                    if t >= 1:
                        ve.wait_ge(t_ps, 2 * t)
                    for qt, (c0, c1) in enumerate(spans):
                        step(dv.tensor_scalar(a_sb[:, c0:c1], s_sb[:, p, 0, c0:c1], att[:, p, 12 + 2 * qt:13 + 2 * qt],
                                             None, ALU.mult))
                    for qt, (c0, c1) in enumerate(spans):
                        settle(1 - qt)
                        last = dv.scalar_tensor_tensor(a_sb[:, c0:c1], s_sb[:, p, 1, c0:c1],
                                                      att[:, p, 13 + 2 * qt:14 + 2 * qt], a_sb[:, c0:c1],
                                                      ALU.mult, ALU.add)
                    last.then_inc(a_ok, 1)
                if pieces[2]:
                    mix_conv(pieces[2])
                if 0 <= g < NH:
                    q = g % 2
                    ve.wait_ge(m_ps, m_no["o", g] + 1)
                    dv.tensor_copy(o_sb[:, q, :, :], bank[7][:, 0:2 * P].rearrange("p (a d) -> p a d", d=P)).then_inc(m_ok, 1)
                    ve.wait_ge(osq_ok, 2 * (g + 1))
                    dv.tensor_scalar(att[:, q, 18:20], att[:, q, 16:18], 1.0 / P, EPS, ALU.mult, ALU.add).then_inc(ovar_ok, 1)
                    ve.wait_ge(ostd_ok, g + 1)
                    step(dv.reciprocal(att[:, q, 22:24], att[:, q, 20:22]))
                    settle()
                    for qt in range(2):
                        last = dv.tensor_scalar(o_sb[:, q, qt, :], o_sb[:, q, qt, :], att[:, q, 22 + qt:23 + qt], None, ALU.mult)
                    last.then_inc(on_ok, 1)
                if f >= 0:
                    ve.wait_ge(m_ps, m_no["n", f] + 1)
                    dv.tensor_scalar(oT[:, f, :], bank[7][:, 0:T], cols[:, R_SUB:R_SUB + 1], 1.0 - LAM_INIT,
                                    ALU.mult, ALU.mult).then_inc(m_ok, 1)
            for n in range(KC):
                ve.wait_ge(proj_ps, IN_SLOTS * 4 + KC + n + 1)
                dv.tensor_tensor(gaT[:, n, :], gaT[:, n, :], bank[n % 4][:, 0:T], ALU.mult).then_inc(mix_ok, 1)
                ve.wait_ge(mix_ok, KC + n + 1)
                dv.tensor_tensor(gaT[:, n, :], gaT[:, n, :], gcT[:, n, :], ALU.add).then_inc(mixed_ok, 1)
            ve.wait_ge(gain_in, 16)
            for t in range(TT):
                for z in range(2):
                    b = 2 * t + z
                    ve.wait_ge(out_ps, b + 1)
                    dv.tensor_tensor(h[:, t, z * FH:(z + 1) * FH], h[:, t, z * FH:(z + 1) * FH], bank[b][:, :],
                                     ALU.add).then_inc(h_ok, 1)
                ve.wait_ge(hsq_ok, t + 1)
                dv.tensor_scalar(st[:, 12 + t:13 + t], st[:, 12 + t:13 + t], 1.0 / D, EPS, ALU.mult,
                                 ALU.add).then_inc(hvar_ok, 1)
                if t == 1:
                    dv.memset(slot[:, :, E:GP], -1.0)
                    dv.memset(gate[:, :, E:GP], 0.0)
                    dv.memset(scat[1], 0.0)
                    dv.memset(y_sb, 0.0).then_inc(ysb_ok, 1)
                ve.wait_ge(hstd_ok, t + 1)
                step(dv.reciprocal(st[:, 16 + t:17 + t], st[:, 14 + t:15 + t]))
                settle()
                dv.scalar_tensor_tensor(hn[:, t, :], h[:, t, :], st[:, 16 + t:17 + t], gain_ffn,
                                        ALU.mult, ALU.mult).then_inc(hn_ok, 1)
            for b in range(4):
                ve.wait_ge(hT_ps, b + 1)
                dv.tensor_copy(hnT[:, b // 2, 4 * (b % 2):4 * (b % 2) + 4, :],
                               bank[4 + b][:, :].rearrange("p (c t) -> p c t", t=P)).then_inc(hT_ok, 1)
            for t in range(TT):
                ve.wait_ge(part0_ok, t + 1)
                ve.wait_ge(hT_ps, 2 * t + 2)
                step(dv.tensor_tensor(hn[:, t, :], hn[:, t, :], hn_parts[0][:, t, :], ALU.subtract))
                settle()
                dv.tensor_copy(hn_parts[1][:, t, :], hn[:, t, :]).then_inc(part1_ok, 1)

            ve.wait_ge(lg_ps, 1)
            for t in range(TT):
                step(dv.tensor_tensor(logits[:, t, :], bank[4][:, t * E:(t + 1) * E], br[:], ALU.add))
            for t in range(TT):
                settle(1)
                step(dv.max(top8[:, t, :], logits[:, t, :]))
            for t in range(TT):
                settle(1)
                step(dv.max_index(idx8[:, t, :], top8[:, t, :], logits[:, t, :]))
                dv.tensor_scalar(rt[:, t, 0:1], top8[:, t, 0:1], -1.0, None, ALU.mult).then_inc(topn_ok, 1)
            settle()
            step(dv.tensor_copy(idxf[:, :, :], idx8[:, :, :]))
            for t in range(TT):
                ve.wait_ge(tope_ok, t + 1)
                step(dv.reciprocal(rt[:, t, 9:10], rt[:, t, 8:9]))
            for t in range(TT):
                settle(1)
                step(dv.tensor_scalar(rt[:, t, 12:16], rt[:, t, 4:8], rt[:, t, 9:10], None, ALU.mult))
            settle()
            for t in range(TT):
                for j in range(TOP_K):
                    last = dv.tensor_scalar(eqs[:, t, j, :], iota2[:, 0, 0:E], idxf[:, t, j:j + 1],
                                           rt[:, t, 12 + j:13 + j], ALU.is_equal, ALU.mult)
                step(last)
            settle()
            for t in range(TT):
                step(dv.tensor_reduce(gate[:, t, 0:E], eqs[:, t, :, :].rearrange("p j e -> p e j"), AX_X, ALU.add))
            settle()
            dv.tensor_scalar(member, gate[:, :, 0:E], 0.0, None, ALU.is_gt).then_inc(memb_ok, 1)
            ve.wait_ge(memb_ok, 1)
            ve.wait_ge(num_ps, 1)
            for t in range(TT):
                step(dv.scalar_tensor_tensor(slot[:, t, 0:E], bank[5][:, t * E:(t + 1) * E], 1.0,
                                            member[:, t, :], ALU.add, ALU.mult))
            step(dv.reduce_max(counts[:, 0:1], bank[5][:, 2 * E:3 * E], AX_X))
            settle(1)
            step(dv.tensor_scalar(slot[:, :, 0:E], slot[:, :, 0:E], -1.0, None, ALU.add))
            settle(1)
            step(dv.tensor_scalar(counts[:, 4:7], thr[:], counts[:, 0:1], None, ALU.is_lt))
            settle()
            step(dv.reduce_sum(counts[:, 8:9], counts[:, 4:7], AX_X))
            settle()
            step(dv.tensor_scalar(counts[:, 9:10], counts[:, 8:9], 1.0, None, ALU.add))
            settle()
            dv.tensor_copy(flag[:], counts[:, 9:10]).then_inc(rounds_ok, 1)
            ve.wait_ge(gT_ps, 1)
            dv.tensor_copy(gateT[0:E, :], bank[6][0:E, 0:T]).then_inc(gT_ok, 1)

            def build(k, par, e, first=False):
                if not first:
                    ve.wait_ge(scatT_ps, k)
                for t in range(TT):
                    dv.tensor_scalar(pick[:, t, :], iota2[:, 0, :], slot[:, t, bass.ds(e, 1)], None, ALU.is_equal)
                    dv.tensor_scalar(gpick[:, t, :, :], iota2[:], slot[:, t, bass.ds(e, 1)],
                                    gate[:, t, bass.ds(e, 1)], ALU.is_equal, ALU.mult)
                dv.tensor_copy(esel[par], eye3[0:3 * E, bass.ds(e, 1)].broadcast_to([3 * E, SLOT])).then_inc(pick_ok, 1)

            def expert(n, k, par, e):
                build(k, 1 - par, e + 1)
                ve.wait_ge(*gu_done(n))
                dv.tensor_scalar(glu_c, bank[4][:, :], LIMIT, None, ALU.min).then_inc(sig_in, 1)
                dv.tensor_scalar(lin_c, bank[5][:, :], LIMIT, -LIMIT, ALU.min, ALU.max).then_inc(gu_read, 1)
                ve.wait_ge(gu_read, n + 2)
                dv.scalar_tensor_tensor(lin_c, lin_c, 1.0, glu_c, ALU.add, ALU.mult).then_inc(lin_ok, 1)
                ve.wait_ge(lin_ok, n + 1)
                ve.wait_ge(sig_ok, n + 1)
                dv.tensor_tensor(act, lin_c, sig, ALU.mult).then_inc(act_ok, 1)

            settle()
            dv.memset(counts[:, 16:17], 0.0).then_inc(gu_read, 1)
            build(0, 0, 0, first=True)
            with ve.Fori(0, E // 2) as i:
                for par in range(2):
                    expert(i * 2 + par, i * 2 + (par + 1), par, i * 2 + par)
            ve.wait_ge(rounds_ok, 1)
            n_rounds = ve.value_load(flag[0:1, 0:1], min_val=1, max_val=T // SLOT)
            with ve.If(n_rounds > 1):
                with ve.Fori(1, n_rounds) as r:
                    ve.wait_ge(pick_ok, r * GP)
                    dv.tensor_scalar(slot[:], slot[:], -float(SLOT), None, ALU.add).then_inc(shift_ok, 1)
                    ve.wait_ge(shift_ok, r)
                    build(r * GP, 0, 0)
                    with ve.Fori(0, E // 2) as i:
                        for par in range(2):
                            expert(r * E + i * 2 + par, r * GP + i * 2 + (par + 1), par, i * 2 + par)
            with ve.Else():
                ve.nop()
            ve.wait_ge(scat_done, n_rounds * E + 1)
            for t in range(TT):
                for z in range(2):
                    dv.tensor_tensor(h[:, t, z * FH:(z + 1) * FH], h[:, t, z * FH:(z + 1) * FH],
                                    bank[2 * t + z][:, :], ALU.add).then_inc(h2_ok, 1)
            ve.wait_ge(fsq_ok, TT)
            dv.tensor_scalar(st[:, 20:22], st[:, 20:22], 1.0 / D, EPS, ALU.mult, ALU.add).then_inc(fvar_ok, 1)
            ve.wait_ge(fstd_ok, 1)
            dv.reciprocal(st[:, 24:26], st[:, 22:24]).then_inc(frec_ok, 1)
            ve.wait_ge(frec_ok, 1)
            ve.wait_ge(gainf_in, 16)
            for t in range(TT):
                dv.scalar_tensor_tensor(fin[:, t, :], h[:, t, :], st[:, 24 + t:25 + t], gain_fin,
                                       ALU.mult, ALU.mult).then_inc(fin_ok, 1)

        @block.tensor
        def _(pe):
            MM, TR = nc.tensor.matmul, nc.tensor.transpose
            pe.wait_ge(const_ok, CONSTS)
            pe.wait_ge(vec_in, 16 * 6)
            pe.wait_ge(taps_in, 32)
            half = TAPS * KC // 2
            TR(bank[7][:, 0:ROWS], rows[0:ROWS, :], ident[0:ROWS, 0:ROWS])
            for a in range(2):
                last = TR(bank[7][:, P + a * half:P + (a + 1) * half], dw_rows[0:half, a, :], ident[0:half, 0:half])
            last.then_inc(vec_ps, 1)
            pe.wait_ge(hs_ok, 3)
            for c in range(KC):
                if c == 7:
                    pe.wait_ge(vec_ok, 1)
                TR(bank[c][:, 0:M], h_norm[0:M, 2, c * P:(c + 1) * P], ident[0:M, 0:M])
                for t in range(TT):
                    last = TR(bank[c][:, M + t * P:M + (t + 1) * P], h_norm[:, t, c * P:(c + 1) * P], ident[:])
                last.then_inc(xT_ps, 1)

            def bank_free(c):
                if c < 4:
                    pe.wait_ge(xT_ok, c + 1)
                elif c - 4 < IN_SLOTS * 4:
                    pe.wait_ge(proj_ok, c - 3)
                else:
                    pe.wait_ge(mix_ok, c - 3 - IN_SLOTS * 4)

            def project(c, src, width):
                s = (c // 4) % RING
                w = ring[:, s, :].rearrange("p (k n) -> p k n", k=KC)
                bank_free(c)
                pe.wait_ge(loaded[s], 16 * (c // 4 // RING + 1))
                for k in range(KC):
                    if c == 0:
                        pe.wait_ge(xT_ok, k + 1)
                    last = MM(bank[c % 4][:, 0:width], w[:, k, (c % 4) * P:(c % 4 + 1) * P], src[:, k, :],
                              start=(k == 0), stop=(k == KC - 1))
                last.then_inc(proj_ps, 1)

            xT_real = xT[:, :, M:L]

            def project_in(c):
                if ORDER[c // 4][0] in (Q, GA, GC):
                    project(c, xT_real, T)
                else:
                    project(c, xT, L)

            def project_conv(n):
                pe.wait_ge(y_ok, KC)
                project(IN_SLOTS * 4 + n, yT, T)

            for c in range(9 * 4):
                project_in(c)
            for c in range(KC):
                pe.wait_ge(conv_ok, c + 1)
                last = MM(bank[6][:, 0:T], ones[:], yT[:, c, :], start=(c == 0), stop=(c == KC - 1))
            last.then_inc(mean_ps, 1)
            for j in range(4):
                project_in(9 * 4 + j)
                for c in (2 * j, 2 * j + 1):
                    pe.wait_ge(csq_ok, c + 1)
                    MM(bank[7][:, 0:T], ones[:], s_sb[:, 0, c % 2, 0:T], start=(c == 0),
                       stop=(c == KC - 1)).then_inc(cvar_ps if c == KC - 1 else csq_used, 1)
            for j in range(4):
                project_in(10 * 4 + j)

            def m_free(key):
                if m_no[key] > 0:
                    pe.wait_ge(m_ok, m_no[key])
                else:
                    pe.wait_ge(cvar_ok, 1)

            for t in range(TICKS):
                g, f = t - 1, t - 2
                if t < NH:
                    pe.wait_ge(proj_ok, run_chunk(K_, t) + 1)
                    if t >= 1:
                        pe.wait_ge(score_read, t)
                    for qt in range(2):
                        c0, n = (0, M + P) if qt == 0 else (M + P, L)
                        for m in range(2):
                            last = MM(score_ps[:, m, c0:c0 + n], qT[m * HD:(m + 1) * HD, t, qt * P:(qt + 1) * P],
                                      kT[m * HD:(m + 1) * HD, t, 0:n], start=True, stop=True)
                    last.then_inc(score_done, 1)
                    m_free(("v", t))
                    pe.wait_ge(proj_ok, run_chunk(V, t) + 1)
                    for b in range(2):
                        TR(bank[7][:, b * P:(b + 1) * P], vT[:, t, M + b * P:M + (b + 1) * P], ident[:])
                    TR(bank[7][0:M, 2 * P:3 * P], vT[:, t, 0:M], ident[:]).then_inc(m_ps, 1)
                for i, piece in enumerate(tick_chunks[t]):
                    if piece:
                        (project_in if piece[0] == "in" else project_conv)(piece[1])
                    if 0 <= g < NH and i < 2:
                        if i == 0:
                            pe.wait_ge(a_ok, g + 1)
                        if 2 * g + i > 0:
                            pe.wait_ge(t_ok, 2 * g + i)
                        c0 = M + P if i == 0 else 0
                        for b in range(2 - i):
                            TR(bank[6][:, b * P:(b + 1) * P], a_sb[:, c0 + M + b * P:c0 + M + (b + 1) * P], ident[:])
                        b = 2 - i
                        TR(bank[6][0:M, b * P:(b + 1) * P], a_sb[:, c0:c0 + M], ident[:]).then_inc(t_ps, 1)
                if 0 <= g < NH:
                    m_free(("o", g))
                    pe.wait_ge(t_ok, 2 * g + 2)
                    for qt, blocks in ((0, ((3, 0), (4, 2))), (1, ((0, 0), (1, 1), (2, 2)))):
                        for i, (b, vb) in enumerate(blocks):
                            n = M if vb == 2 else P
                            last = MM(bank[7][:, qt * P:(qt + 1) * P], aT[0:n, b, :], v_tok[0:n, vb, g, :],
                                      start=(i == 0), stop=(i == len(blocks) - 1))
                    last.then_inc(m_ps, 1)
                if f >= 0:
                    m_free(("n", f))
                    pe.wait_ge(on_ok, f + 1)
                    for qt in range(2):
                        last = TR(bank[7][:, qt * P:(qt + 1) * P], o_sb[:, f % 2, qt, :], ident[:])
                    last.then_inc(m_ps, 1)
            pe.wait_ge(m_ok, len(m_seq))
            for n in range(KC):
                project(IN_SLOTS * 4 + KC + n, oT, T)
            for b in range(4):
                t, z = divmod(b, 2)
                pe.wait_ge(mix_ok, KC + 4 + b + 1)
                for k in range(KC):
                    n = TRUNK - 2 + k // 4
                    if b == 0:
                        pe.wait_ge(mixed_ok, k + 1)
                        pe.wait_ge(loaded[n % RING], 16 * (n // RING + 1))
                    w = ring[:, n % RING, :].rearrange("p (k n) -> p k n", k=4)
                    last = MM(bank[b][:, :], gaT[:, k, t * P:(t + 1) * P], w[:, k % 4, z * FH:(z + 1) * FH],
                              start=(k == 0), stop=(k == KC - 1))
                last.then_inc(out_ps, 1)
            for b in range(4):
                t = b // 2
                pe.wait_ge(hn_ok, t + 1)
                for c in range(4 * (b % 2), 4 * (b % 2) + 4):
                    last = TR(bank[4 + b][:, (c % 4) * P:(c % 4 + 1) * P], hn[:, t, c * P:(c + 1) * P], ident[:])
                last.then_inc(hT_ps, 1)
            pe.wait_ge(hT_ok, 4)
            pe.wait_ge(small_in, 32)
            for t in range(TT):
                for c in range(KC):
                    last = MM(bank[4][:, t * E:(t + 1) * E], hnT[:, t, c, :], wr[:, c, :], start=(c == 0), stop=(c == KC - 1))
            last.then_inc(lg_ps, 1)
            pe.wait_ge(memb_ok, 1)
            MM(bank[5][:, 0:E], before[:], member[:, 0, :], start=True, stop=True)
            MM(bank[5][:, E:2 * E], ones[:], member[:, 0, :], start=True, stop=False)
            MM(bank[5][:, E:2 * E], before[:], member[:, 1, :], start=False, stop=True)
            MM(bank[5][:, 2 * E:3 * E], ones[:], member[:, 0, :], start=True, stop=False)
            MM(bank[5][:, 2 * E:3 * E], ones[:], member[:, 1, :], start=False, stop=True).then_inc(num_ps, 1)
            for t in range(TT):
                last = TR(bank[6][0:E, t * P:(t + 1) * P], gate[:, t, 0:E], ident[:])
            last.then_inc(gT_ps, 1)
            pe.wait_ge(gT_ok, 1)
            pe.wait_ge(bdn_in, 16)
            for t in range(TT):
                for z in range(2):
                    MM(bank[2 * t + z][:, :], gateT[0:E, t * P:(t + 1) * P], bias_dn[0:E, z * FH:(z + 1) * FH],
                       start=True, stop=True)

            def prepare(n, k):
                pe.wait_ge(pick_ok, k + 1)
                pe.wait_ge(ysb_ok, n + 1)
                for c in range(KC):
                    for i in range(3 * TT):
                        last = MM(bank[6][:, c * SLOT:(c + 1) * SLOT], hn_parts[i // TT][:, i % TT, c * P:(c + 1) * P],
                                  pick[:, i % TT, :], start=(i == 0), stop=(i == 3 * TT - 1))
                last.then_inc(gather_ps, 1)
                for t in range(TT):
                    last = TR(bank[7][:, t * P:(t + 1) * P], gpick[:, t, :, :].rearrange("p z s -> p (z s)"), ident[:])
                last.then_inc(scatT_ps, 1)

            def scatter(n, par):
                pe.wait_ge(ysb_ok, n + 1)
                for t in range(TT):
                    for z in range(2):
                        last = MM(bank[2 * t + z][:, :], scat[par][z * SLOT:(z + 1) * SLOT, t * P:(t + 1) * P],
                                  y_sb[z * SLOT:(z + 1) * SLOT, :], start=False, stop=True, skip_group_check=True)
                last.then_inc(scat_done, 1)

            def expert(n, k, par):
                pe.wait_ge(xg_ok, k)
                pe.wait_ge(gu_read, n + 1)
                for b in range(2):
                    for z in range(2):
                        q = 2 * b + z
                        MM(bank[4 + b][z * SLOT:(z + 1) * SLOT, :], esel[par], bias_gu[:, q * FH:(q + 1) * FH],
                           start=True, stop=False)
                for j in range(4):
                    s = moe_slot(j)
                    pe.wait_ge(loaded[s], (n + (uses(s) + 1)) * 16)
                    w = ring[:, s, :].rearrange("p (k n) -> p k n", k=2)
                    for kk in range(2):
                        c = 2 * j + kk
                        for b in range(2):
                            for z in range(2):
                                q = 2 * b + z
                                last = MM(bank[4 + b][z * SLOT:(z + 1) * SLOT, :], xg[par][:, c, :],
                                          w[:, kk, q * FH:(q + 1) * FH], start=False, stop=(c == KC - 1))
                    last.then_inc(freed[s], 1)
                pe.wait_ge(scatT_ok, k)
                scatter(n, 1 - par)
                prepare(n, k)
                pe.wait_ge(act_ok, n + 1)
                pe.wait_ge(scatT_ok, k + 1)
                for b in range(4):
                    last = TR(bank[7][:, b * P:(b + 1) * P], act[:, b * P:(b + 1) * P], ident[:])
                last.then_inc(actT_ps, 1)
                pe.wait_ge(actT_ok, n + 1)
                pe.wait_ge(xg_ok, k + 1)
                for j in range(4, 6):
                    s = moe_slot(j)
                    pe.wait_ge(loaded[s], (n + (uses(s) + 1)) * 16)
                    w = ring[:, s, :].rearrange("p (k n) -> p k n", k=4)
                    for kk in range(4):
                        for z in range(2):
                            last = MM(bank[6][z * SLOT:(z + 1) * SLOT, :], actT[:, kk, j - 4, :],
                                      w[:, kk, z * FH:(z + 1) * FH], start=(j == 4 and kk == 0), stop=(j == 5 and kk == 3))
                    last.then_inc(freed[s], 1)

            pe.wait_ge(part2_ok, TT)
            prepare(0, 0)
            pe.wait_ge(pool, 13)
            with pe.Fori(0, E // 2) as i:
                for par in range(2):
                    expert(i * 2 + par, i * 2 + (par + 1), par)
            pe.wait_ge(rounds_ok, 1)
            n_rounds = pe.value_load(flag[0:1, 0:1], min_val=1, max_val=T // SLOT)
            with pe.If(n_rounds > 1):
                with pe.Fori(1, n_rounds) as r:
                    prepare(r * E, r * GP)
                    with pe.Fori(0, E // 2) as i:
                        for par in range(2):
                            expert(r * E + i * 2 + par, r * GP + i * 2 + (par + 1), par)
            with pe.Else():
                pe.nop()
            scatter(n_rounds * E, 1)


_INS = ["x", "meta_tokens", "norm_mix", "w_in", "b_in", "lam_params", "subln_gain", "w_attn_proj",
        "conv_dw_w", "conv_dw_b", "conv_ln_g", "conv_ln_b", "w_conv_proj", "w_out", "norm_ffn",
        "w_router", "b_router", "w_gate_up", "b_gate_up", "w_down", "b_down", "norm_final"]


def kernel(**inputs):
    import concourse.bacc as bacc
    import numpy as np
    from concourse.bass_utils import run_bass_kernel_spmd

    nc = bacc.Bacc("TRN2", target_bir_lowering=False, num_devices=1)
    arrays, args = {}, []
    for name in _INS:
        a = np.ascontiguousarray(inputs[name])
        arrays[f"in_{name}"] = a
        args.append(nc.dram_tensor(f"in_{name}", a.shape, F32, kind="ExternalInput").ap())
    args.append(nc.dram_tensor("out", inputs["x"].shape, F32, kind="ExternalOutput").ap())
    encoder_block(nc, *args)
    r = run_bass_kernel_spmd(nc, [arrays], core_ids=[0])
    return r.results[0]["out"]
```

```python
import math
from contextlib import ExitStack

import concourse.bass as bass
from concourse import mybir

P = 128
BF16 = mybir.dt.bfloat16
F32R = mybir.dt.float32r
F32 = mybir.dt.float32
I32 = mybir.dt.int32
U32 = mybir.dt.uint32
ALU = mybir.AluOpType
ACT = mybir.ActivationFunctionType
AX_X = mybir.AxisListType.X

CHUNK = 64
TOP_K = 4
ALPHA = 1.702
LIMIT = 7.0
EPS = 1e-5
LAM_INIT = 0.8 - 0.6 * math.exp(-0.3 * 0)
FAR = 1e30
RING = 8
TRING = 3
WIDE = 4096


def encoder_block(nc, x, meta, norm_mix, w_in, b_in, lam_params, subln, w_attn, dw_w, dw_b,
                  ln_g, ln_b, w_conv, w_out, norm_ffn, w_router, b_router, w_gu, b_gu,
                  w_dn, b_dn, norm_final, out):
    D = x.shape[2]
    T = x.shape[1]
    M = meta.shape[0]
    L = M + T
    KC = D // P
    TT = T // P
    NH = D // P
    HD = 64
    E = w_router.shape[2]
    TAPS = dw_w.shape[1]
    PAD = TAPS - 1 - M
    SLOT = 64
    FH = D // 2
    SCALE = HD ** -0.5
    IN_SLOTS = w_in.shape[2] // 512
    assert (D, T, M, E, TAPS) == (1024, 256, 16, 32, 31)

    Q, K_, V, CA, CB, GA, GC = range(7)
    ORDER = [(CA, 0), (CB, 0), (CA, 1), (CB, 1), (GA, 0), (GC, 0), (GA, 1), (GC, 1),
             (Q, 0), (K_, 0), (V, 0), (Q, 1), (K_, 1), (V, 1)]
    assert len(ORDER) == IN_SLOTS
    TRUNK = IN_SLOTS + 6
    PER_EXPERT = 6

    UNROLL = RING * PER_EXPERT // math.gcd(RING, PER_EXPERT) // PER_EXPERT
    GROUPS = E // UNROLL

    def trunk_slot(n):
        return (n - TRUNK) % TRING if n < TRUNK - 1 else TRING

    def moe_slot(m, j):
        return (TRING - 1 + PER_EXPERT * m + j) % RING

    def moe_turn(g, m, j):
        return PER_EXPERT * UNROLL // RING * g + (PER_EXPERT * m + j) // RING

    R_BIN, R_MIX = 0, w_in.shape[2] // P
    R_DWB = R_MIX + KC
    R_LNG = R_DWB + KC
    R_LNB = R_LNG + KC
    R_SUB = R_LNB + KC
    ROWS = R_SUB + 1

    with ExitStack() as ctx:
        def sb(name, shape, dt=F32):
            return ctx.enter_context(nc.sbuf_tensor(name, shape, dt))

        def sem(name):
            return ctx.enter_context(nc.semaphore(name))

        bank = [ctx.enter_context(nc.psum_tensor(f"bank{i}", [P, 512], F32)) for i in range(4)]
        score_ps = ctx.enter_context(nc.psum_tensor("score_ps", [P, 2, 512], F32))
        bank += [score_ps[:, 0, :], score_ps[:, 1, :]]
        bank += [ctx.enter_context(nc.psum_tensor(f"bank{i}", [P, 512], F32)) for i in (6, 7)]

        SW = M + P + L
        base = (nc.sbuf_base + 63) // 64 * 64

        def at(name, offset, shape, dt=F32):
            t = nc.alloc_sbuf_tensor_at(name, shape, dt, offset=base + 4 * offset)
            words = -(-math.prod(shape[1:]) * (2 if dt == BF16 else 4) // 4)
            return t[:], (offset + words + 7) // 8 * 8

        ring, R1 = at("ring", 0, [P, RING, WIDE])
        woh, _ = at("woh", (RING - 2) * WIDE, [P, KC, D], F32R)
        wol0, _ = at("wol0", trunk_slot(TRUNK - 2) * WIDE, [P, KC // 2, D], F32R)
        wol1, _ = at("wol1", trunk_slot(TRUNK - 1) * WIDE, [P, KC // 2, D], F32R)
        wol = [[wol0, wol1][k // 4][:, k % 4, :] for k in range(KC)]
        yh, e0 = at("yh", TRING * WIDE, [P, KC, T], F32R)
        yl, e0 = at("yl", e0, [P, KC, T], F32R)
        h_norm, _ = at("h_norm", e0, [P, 3, D])
        v_tok, e0 = at("v_tok", e0, [P, 3, NH, P])
        vT, e0 = at("vT", e0, [P, NH, L])
        xh, e0 = at("xh", e0, [P, KC, L], F32R)
        xl, e0 = at("xl", e0, [P, KC, L], F32R)
        s0 = e0
        s_sb, e0 = at("s_sb", e0, [P, 2, 2, SW])
        a_sb, e0 = at("a_sb", e0, [P, SW])
        aT, e0 = at("aT", e0, [P, 5, P])
        o_sb, e0 = at("o_sb", e0, [P, 4, 2, P])
        dist, e0 = at("dist", e0, [P, SW])
        qT, e0 = at("qT", e0, [P, NH, T])
        junk, e0 = at("junk", e0, [P, 2, P])
        att, e0 = at("att", e0, [P, 2, 32])
        osq, e0 = at("osq", e0, [P, 3, 4, 2])
        assert e0 <= R1
        rows, e1 = at("rows", s0, [P, P])
        dw_rows, e1 = at("dw_rows", e1, [P, 2, P])
        lam_in, e1 = at("lam_in", e1, [P, 4, HD])
        kT, R2 = at("kT", R1, [P, NH, L])
        bias_f32, _ = at("bias_f32", R1, [3 * E, 2 * D])
        glu_c, e1 = at("glu_c", R1, [P, FH])
        lin_c, e1 = at("lin_c", e1, [P, FH])
        sig, e1 = at("sig", e1, [P, FH])
        act, e1 = at("act", e1, [P, FH])
        assert e1 <= R2
        fin, _ = at("fin", R1, [P, TT, D])
        u, R3 = at("u", R2, [P, KC, PAD + L])
        squares, e1 = at("squares", R2, [P, 2, T])
        mean, e1 = at("mean", e1, [P, T])
        std, _ = at("std", e1, [P, T])
        oh, _ = at("oh", R2, [P, NH, T], F32R)
        hn, _ = at("hn", R2, [P, TT, D])
        gain_fin, _ = at("gain_fin", R2, [P, D])
        cbT, R4 = at("cbT", R3, [P, KC, L])
        yT, _ = at("yT", R3, [P, KC, T])
        ol, _ = at("ol", R3, [P, NH, T], F32R)
        parts0, e1 = at("parts0", R3, [P, 2, D], BF16)
        bias_dn, e1 = at("bias_dn", e1, [E, D])
        gaT, R5 = at("gaT", R4, [P, KC, T])
        gcT, R6 = at("gcT", R5, [P, KC, T])
        ml, _ = at("ml", R4, [P, KC, T], F32R)
        mh, _ = at("mh", R5, [P, KC, T], F32R)
        parts1, e1 = at("parts1", R4, [P, 3, D], BF16)
        actT, e1 = at("actT", e1, [P, 4, 2, SLOT])
        assert e1 <= R5
        third0, e1 = at("third0", R5, [P, D], BF16)
        parts = [[parts0[:, 0, :], parts0[:, 1, :], third0], [parts1[:, i, :] for i in range(3)]]
        y_sb, e1 = at("y_sb", e1, [P, FH])
        assert e1 <= R6
        wh0, e1 = at("wh0", R6, [P, KC, P], F32R)
        wh1, e1 = at("wh1", e1, [P, KC, P], F32R)
        wl0, e1 = at("wl0", e1, [P, KC, P], F32R)
        wl1, R7 = at("wl1", e1, [P, KC, P], F32R)
        wh, wl = [wh0, wh1], [wl0, wl1]
        hnT, e1 = at("hnT", R6, [P, TT, KC, P])
        xg0, e2 = at("xg0", R6, [P, KC, SLOT])
        xg1, e2 = at("xg1", e2, [P, KC, SLOT])
        xg = [xg0, xg1]
        GP = E + 1
        scat0, e1 = at("scat0", e1, [P, T])
        scat1, e1 = at("scat1", e1, [P, T])
        scat = [scat0, scat1]
        pick, e1 = at("pick", e1, [P, TT, SLOT], BF16)
        gpick, e1 = at("gpick", e1, [P, TT, 2, SLOT])
        esel0, e1 = at("esel0", e1, [3 * E, SLOT], BF16)
        esel1, e1 = at("esel1", e1, [3 * E, SLOT], BF16)
        esel = [esel0, esel1]
        gate, e1 = at("gate", e1, [P, TT, GP])
        slot, e1 = at("slot", e1, [P, TT, GP])
        member, e1 = at("member", e1, [P, TT, E], BF16)
        eqs, e1 = at("eqs", e1, [P, TT, TOP_K, E])
        logits, e1 = at("logits", e1, [P, TT, E])
        gateT, e1 = at("gateT", e1, [E, T])
        counts, e1 = at("counts", e1, [P, 16])
        top8, e1 = at("top8", e1, [P, TT, 8])
        idx8, e1 = at("idx8", e1, [P, TT, 8], U32)
        idxf, e1 = at("idxf", e1, [P, TT, 8])
        assert e1 <= R7
        h_meta, _ = at("h_meta", R7, [P, D])
        bias_gu, R8 = at("bias_gu", R7, [3 * E, 2 * D], BF16)
        h, R8 = at("h", R8, [P, TT, D])
        gain_ffn, R8 = at("gain_ffn", R8, [P, D])
        ident, R8 = at("ident", R8, [P, P])
        eye3, R8 = at("eye3", R8, [P, E + 2], BF16)
        ones, R8 = at("ones", R8, [P, P])
        ones_bf, R8 = at("ones_bf", R8, [P, P], BF16)
        before, R8 = at("before", R8, [P, P], BF16)
        iota2, R8 = at("iota2", R8, [P, 2, SLOT])
        thr, R8 = at("thr", R8, [P, 3])
        cols, R8 = at("cols", R8, [P, ROWS + 1])
        taps, R8 = at("taps", R8, [P, TAPS * KC])
        wr, R8 = at("wr", R8, [P, KC, E])
        br, R8 = at("br", R8, [P, E])
        st, R8 = at("st", R8, [P, 32])
        rt, R8 = at("rt", R8, [P, 2, 32])
        flag, R8 = at("flag", R8, [P, 1], I32)
        sb("arena", [P, R8 + 16])

        loaded = [sem(f"loaded{s}") for s in range(RING)]
        freed = [sem(f"freed{s}") for s in range(RING)]
        x_in = [sem(f"x_in{t}") for t in range(3)]
        vec_in, lam_ld, small_in, taps_in = sem("vec_in"), sem("lam_ld"), sem("small_in"), sem("taps_in")
        gain_in, gainf_in, bdn_in, bgu_in = sem("gain_in"), sem("gainf_in"), sem("bdn_in"), sem("bgu_in")
        const_ok = sem("const_ok")
        sq_ok, rs_ok, var_ok, hs_ok = sem("sq_ok"), sem("rs_ok"), sem("var_ok"), sem("hs_ok")
        vec_ps, vec_ok = sem("vec_ps"), sem("vec_ok")
        xT_ps, xh_ok, xh_dve, xT_ok = sem("xT_ps"), sem("xh_ok"), sem("xh_dve"), sem("xT_ok")
        wh_ok, wh_used, wl_ok = sem("wh_ok"), sem("wh_used"), sem("wl_ok")
        yh_ok, yl_ok = sem("yh_ok"), sem("yl_ok")
        proj_ps, proj_ok = sem("proj_ps"), sem("proj_ok")
        dve = sem("dve")
        pool = sem("pool")
        conv_ok = sem("conv_ok")
        mean_ps, cen_ok, csq_ok, csq_used, cvar_ps = [sem(n) for n in ("mean_ps", "cen_ok", "csq_ok", "csq_used", "cvar_ps")]
        cvar_ok, cstd_ok, z_ok, y_ok = [sem(n) for n in ("cvar_ok", "cstd_ok", "z_ok", "y_ok")]
        lam_arg, lam_exp = sem("lam_arg"), sem("lam_exp")
        score_done, score_read, negmax_ok, exp_ok = [sem(n) for n in ("score_done", "score_read", "negmax_ok", "exp_ok")]
        a_ok, t_ps, t_ok = sem("a_ok"), sem("t_ps"), sem("t_ok")
        m_ps, m_ok = sem("m_ps"), sem("m_ok")
        osq_ok, ovar_ok, ostd_ok, on_ok, oh_ok = [sem(n) for n in ("osq_ok", "ovar_ok", "ostd_ok", "on_ok", "oh_ok")]
        woh_ok, wol_ok, mh_ok, ml_ok = [sem(n) for n in ("woh_ok", "wol_ok", "mh_ok", "ml_ok")]
        mix_ok, mixed_ok = sem("mix_ok"), sem("mixed_ok")
        out_ps, h_ok, hsq_ok, hvar_ok, hstd_ok, hn_ok = [sem(n) for n in ("out_ps", "h_ok", "hsq_ok", "hvar_ok", "hstd_ok", "hn_ok")]
        hT_ps, hT_ok, lg_ps, topn_ok, tope_ok, memb_ok = [sem(n) for n in ("hT_ps", "hT_ok", "lg_ps", "topn_ok", "tope_ok", "memb_ok")]
        num_ps, gT_ps, gT_ok, rounds_ok, zero_ok = [sem(n) for n in ("num_ps", "gT_ps", "gT_ok", "rounds_ok", "zero_ok")]
        pick_ok, gather_ps, xg_ok, scatT_ps, scatT_ok = [sem(n) for n in ("pick_ok", "gather_ps", "xg_ok", "scatT_ps", "scatT_ok")]
        bias_dve, off_ok = sem("bias_dve"), sem("off_ok")
        part0_ok, part2_ok = sem("part0_ok"), sem("part2_ok")
        gu_read, sig_in, sig_ok, lin_ok, act_ok, shift_ok = [sem(n) for n in ("gu_read", "sig_in", "sig_ok", "lin_ok", "act_ok", "shift_ok")]
        actT_ps, actT_ok, ysb_ok, scat_done, acc_ok = [sem(n) for n in ("actT_ps", "actT_ok", "ysb_ok", "scat_done", "acc_ok")]
        h2_ok, fsq_ok, fvar_ok, fstd_ok, frec_ok, fin_ok, stored = [sem(n) for n in (
            "h2_ok", "fsq_ok", "fvar_ok", "fstd_ok", "frec_ok", "fin_ok", "stored")]

        block = ctx.enter_context(nc.Block())

        TICKS = NH + 1

        def turns(t):
            return (0, 1) if t == 5 else ()

        LATE0 = 11 * 4
        late = [("in", c) for c in range(LATE0, IN_SLOTS * 4)] + [("conv", n) for n in range(KC)]
        tick_chunks = []
        for t in range(TICKS):
            n = 4 if t == 0 else 2 if t < 8 else 0
            piece, late = late[:n], late[n:]
            tick_chunks.append([piece[i] if i < len(piece) else None for i in range(max(n, 2))])
        tail_chunks, late = late[:2], late[2:]
        assert not late

        def run_chunk(kind, n):
            return ORDER.index((kind, n // 4)) * 4 + n % 4

        def place(piece):
            return piece[1] + (IN_SLOTS * 4 if piece[0] == "conv" else 0)

        def load_no(n):
            return sum(trunk_slot(i) == trunk_slot(n) for i in range(n + 1))

        def uses(s):
            return sum(trunk_slot(n) == s for n in range(TRUNK))

        SPLIT = TRUNK - 2

        def gu_done(g, m):
            return freed[moe_slot(m, 3)], moe_turn(g, m, 3) + 1

        def y_done(g, m):
            return freed[moe_slot(m, 5)], moe_turn(g, m, 5) + 1

        m_seq = []
        for t in range(TICKS):
            m_seq += [("v", t)] * (t < NH) + [("n", f) for f in turns(t)] + [("o", t - 1)] * (t > 0)
        m_seq += [("n", 2), ("n", 3)]
        m_no = {key: i for i, key in enumerate(m_seq)}

        def chunk_of(c):
            w = ring[:, trunk_slot(c // 4), :].rearrange("p (k n) -> p k n", k=KC)
            return w[:, :, (c % 4) * P:(c % 4 + 1) * P]

        def w_out_rows(k):
            w = ring[:, trunk_slot(SPLIT + k // 4), :].rearrange("p (k n) -> p k n", k=4)
            return w[:, k % 4, :]

        @block.sync
        def _(sp):
            for t in range(TT):
                sp.dma_start(h[:, t, :], x[0, t * P:(t + 1) * P, :]).then_inc(x_in[t], 16)
            for r0, src in ((R_BIN, b_in), (R_MIX, norm_mix), (R_DWB, dw_b), (R_LNG, ln_g), (R_LNB, ln_b), (R_SUB, subln)):
                n = src.shape[1] // P
                sp.dma_start(rows[r0:r0 + n, :], src.rearrange("a (r p) -> (a r) p", p=P)).then_inc(vec_in, 16)
            taps_rows = dw_w[0].rearrange("k (c p) -> (k c) p", p=P)
            half = TAPS * KC // 2
            for a in range(2):
                sp.dma_start(dw_rows[0:half, a, :], taps_rows[a * half:(a + 1) * half, :]).then_inc(taps_in, 16)

            def group(w, c0):
                return w[0, :, c0:c0 + 512].rearrange("(k p) n -> p k n", p=P)

            sources = [group(w_in, (kind * 2 + half) * 512) for kind, half in ORDER]
            sources += [group(w_conv, 0), group(w_conv, 512), group(w_attn, 0), group(w_attn, 512)]
            sources += [w_out[0, a * FH:(a + 1) * FH, :].rearrange("(k p) n -> p k n", p=P) for a in range(2)]
            for n, src in enumerate(sources):
                if n == TRUNK - 1:
                    sp.wait_ge(proj_ps, IN_SLOTS * 4 + KC)
                elif n >= TRING:
                    sp.wait_ge(wl_ok, 4 * (n - TRING + 1))
                s = trunk_slot(n)
                sp.dma_start(ring[:, s, :].rearrange("p (k n) -> p k n", k=src.shape[1]), src).then_inc(loaded[s], 16)
            sp.wait_ge(score_done, NH)
            for j in range(3):
                sp.dma_start(bias_f32[j * E:(j + 1) * E, :], b_gu[0]).then_inc(bgu_in, 16)

            def slot_empty(s):
                if s in (trunk_slot(SPLIT - 2), trunk_slot(SPLIT - 1)):
                    last = SPLIT - 2 if s == trunk_slot(SPLIT - 2) else SPLIT - 1
                    sp.wait_ge(wl_ok, 4 * (last + 1))
                elif s in (4, 5):
                    sp.wait_ge(m_ok, len(m_seq))
                else:
                    sp.wait_ge(out_ps, 2 * TT)

            def load(g, m, j, e):
                s, turn = moe_slot(m, j), moe_turn(g, m, j)
                if isinstance(turn, int) and turn == 0:
                    slot_empty(s)
                else:
                    sp.wait_ge(freed[s], turn)
                if j < 4:
                    src = w_gu[0, bass.ds(e, 1), j * 256:(j + 1) * 256, :]
                    kk = 2
                else:
                    src = w_dn[0, bass.ds(e, 1), (j - 4) * 512:(j - 3) * 512, :]
                    kk = 4
                sp.dma_start(ring[:, s, :].rearrange("p (k n) -> p k n", k=kk),
                             src.rearrange("a (k p) n -> p (a k) n", p=P)).then_inc(loaded[s], 16)

            def load_expert(g, m, e):
                for j in range(PER_EXPERT):
                    load(g, m, j, e)

            for q in (0, 2, 3, 6, 1, 4, 5, 7):
                m, j = divmod(q, PER_EXPERT)
                if q == 6:
                    sp.wait_ge(proj_ps, IN_SLOTS * 4 + 2 * KC)
                    sp.dma_start(bias_dn, b_dn[0]).then_inc(bdn_in, 16)
                load(0, m, j, m)
            for q in range(RING, PER_EXPERT * UNROLL):
                m, j = divmod(q, PER_EXPERT)
                load(0, m, j, m)
            with sp.Fori(1, GROUPS) as i:
                for m in range(UNROLL):
                    load_expert(i, m, i * UNROLL + m)
            sp.wait_ge(rounds_ok, 1)
            n_rounds = sp.value_load(flag[0:1, 0:1], min_val=1, max_val=T // SLOT)
            with sp.If(n_rounds > 1):
                with sp.Fori(1, n_rounds) as r:
                    with sp.Fori(0, GROUPS) as i:
                        for m in range(UNROLL):
                            load_expert(r * GROUPS + i, m, i * UNROLL + m)
            with sp.Else():
                sp.nop()
            for t in range(TT):
                sp.wait_ge(fin_ok, t + 1)
                sp.dma_start(out[0, t * P:(t + 1) * P, :], fin[:, t, :]).then_inc(stored, 16)
            sp.wait_ge(stored, 16 * TT)

        @block.gpsimd
        def _(gp):
            nc.gpsimd.memset(ident[:], 0.0).then_inc(pool, 1)
            nc.gpsimd.memset(ones[:], 1.0).then_inc(pool, 1)
            nc.gpsimd.memset(eye3[:], 0.0).then_inc(pool, 1)
            nc.gpsimd.memset(ones_bf[:], 1.0).then_inc(pool, 1)
            gp.wait_ge(pool, 4)
            nc.gpsimd.affine_select(out=ident[:], in_=ident[:], compare_op=ALU.not_equal, fill=1.0, base=0,
                                    pattern=[[-1, P]], channel_multiplier=1).then_inc(const_ok, 1)
            nc.gpsimd.affine_select(out=before[:], in_=ones_bf[:], compare_op=ALU.is_gt, fill=0.0, base=0,
                                    pattern=[[1, P]], channel_multiplier=-1).then_inc(const_ok, 1)
            nc.gpsimd.iota(iota2[:], [[0, 2], [1, SLOT]], base=0, channel_multiplier=0,
                           allow_small_or_imprecise_dtypes=True).then_inc(const_ok, 1)
            nc.gpsimd.iota(thr[:], [[SLOT, 3]], base=SLOT, channel_multiplier=0,
                           allow_small_or_imprecise_dtypes=True).then_inc(const_ok, 1)
            nc.gpsimd.iota(dist[:, 0:M + P], [[-1, M + P]], base=M, channel_multiplier=1,
                           allow_small_or_imprecise_dtypes=True).then_inc(const_ok, 1)
            nc.gpsimd.iota(dist[:, M + P:SW], [[-1, L]], base=M + P, channel_multiplier=1,
                           allow_small_or_imprecise_dtypes=True).then_inc(const_ok, 1)
            for j in range(3):
                if j:
                    gp.wait_ge(pool, 4 + j)
                nc.gpsimd.affine_select(out=eye3[:], in_=eye3[:], compare_op=ALU.not_equal, fill=1.0, base=-E * j,
                                        pattern=[[-1, E + 2]], channel_multiplier=1).then_inc(pool, 1)
            gp.dma_start(lam_in, lam_params[0].partition_broadcast(P)).then_inc(lam_ld, 16)
            gp.dma_start(wr[:], w_router[0].rearrange("(c p) e -> p c e", p=P)).then_inc(small_in, 16)
            gp.dma_start(br[:], b_router[0].partition_broadcast(P)).then_inc(small_in, 16)
            for c in range(SPLIT * 4):
                gp.wait_ge(wh_ok, c + 1)
                if c >= 2:
                    gp.wait_ge(proj_ps, c - 1)
                nc.gpsimd.tensor_tensor(wl[c % 2], chunk_of(c), wh[c % 2].bitcast(F32), ALU.subtract).then_inc(wl_ok, 1)
                if c == 8:
                    gp.dma_start(gain_ffn, norm_ffn[0].partition_broadcast(P)).then_inc(gain_in, 16)
                if c in (IN_SLOTS * 4 - 2, IN_SLOTS * 4 - 1):
                    for k in range(4 * (c % 2), 4 * (c % 2) + 4):
                        gp.wait_ge(yh_ok, k + 1)
                        nc.gpsimd.tensor_tensor(yl[:, k, :], yT[:, k, :], yh[:, k, :].bitcast(F32),
                                                ALU.subtract).then_inc(yl_ok, 1)
            def bias_off(q):
                r = slice(q * E, (q + 1) * E)
                nc.gpsimd.tensor_tensor(bias_f32[r, :], bias_f32[r, :], bias_gu[r, :], ALU.subtract).then_inc(off_ok, 1)

            gp.wait_ge(bias_dve, 1)
            bias_off(1)
            bias_off(2)
            gp.wait_ge(bias_dve, 3)
            bias_off(2)
            gp.wait_ge(off_ok, 3)
            gp.wait_ge(part0_ok, 2)
            gp.wait_ge(hT_ps, 4)
            nc.gpsimd.tensor_tensor(hn[:, 1, :], hn[:, 1, :], parts[1][0], ALU.subtract).then_inc(pool, 1)
            gp.wait_ge(pool, 8)
            nc.gpsimd.tensor_copy(parts[1][1], hn[:, 1, :]).then_inc(pool, 1)
            gp.wait_ge(pool, 9)
            nc.gpsimd.tensor_tensor(parts[1][2], hn[:, 1, :], parts[1][1], ALU.subtract).then_inc(part2_ok, 1)
            gp.wait_ge(part2_ok, TT)
            gp.dma_start(gain_fin, norm_final.partition_broadcast(P)).then_inc(gainf_in, 16)

        CONSTS = 6
        XH_DVE = 4

        @block.scalar
        def _(act_e):
            A = nc.scalar.activation
            act_e.dma_start(h_meta[0:M, :], meta).then_inc(x_in[2], 16)
            act_e.wait_ge(zero_ok, 1)
            A(st[:, 26:27], st[:, 27:28], ACT.Sqrt)
            for t in range(3):
                act_e.wait_ge(x_in[t], 16)
                src = h[:, t, :] if t < 2 else h_meta[0:M, :]
                n = P if t < 2 else M
                A(h_norm[0:n, t, :], src, ACT.Square, accum_out=st[0:n, t:t + 1]).then_inc(sq_ok, 1)
            act_e.wait_ge(var_ok, 1)
            A(st[:, 3:6], st[:, 0:3], ACT.Sqrt).then_inc(rs_ok, 1)

            def evacuate(c):
                kind, hf = ORDER[c // 4]
                n = hf * 4 + c % 4
                dst = {Q: qT[:, n, :], K_: kT[:, n, :], V: vT[:, n, :], CA: u[:, n, PAD:PAD + L],
                       CB: cbT[:, n, :], GA: gaT[:, n, :], GC: gcT[:, n, :]}[kind]
                fn = ACT.Sigmoid if kind in (CB, GA, GC) else ACT.Identity
                width = T if kind in (Q, GA, GC) else L
                col = R_BIN + kind * KC + n
                act_e.wait_ge(proj_ps, c + 1)
                A(dst, bank[c % 4][:, 0:width], fn, bias=cols[:, col:col + 1]).then_inc(proj_ok, 1)

            def split(c):
                act_e.wait_ge(loaded[trunk_slot(c // 4)], 16 * load_no(c // 4))
                if c >= 2:
                    act_e.wait_ge(wh_used, c - 1)
                    act_e.wait_ge(wl_ok, c - 1)
                nc.scalar.copy(wh[c % 2], chunk_of(c)).then_inc(wh_ok, 1)

            split(0)
            act_e.wait_ge(vec_ok, 1)
            for c in range(XH_DVE, KC):
                if c == KC - 1:
                    split(1)
                act_e.wait_ge(xT_ps, c + 1)
                A(xh[:, c, :], bank[c][:, 0:L], ACT.Identity, scale=cols[:, R_MIX + c:R_MIX + c + 1]).then_inc(xh_ok, 1)
            for c in range(LATE0):
                split(c + 2)
                evacuate(c)
            act_e.wait_ge(lam_arg, 1)
            A(st[:, 8:10], st[:, 6:8], ACT.Exp).then_inc(lam_exp, 1)
            def exponentials(t):
                p = t % 2
                act_e.wait_ge(negmax_ok, t + 1)
                for m in range(2):
                    for qt, (c0, c1) in enumerate(((0, M + P), (M + P, SW))):
                        z = 8 + 2 * qt + m
                        A(s_sb[:, p, m, c0:c1], s_sb[:, p, m, c0:c1], ACT.Exp, scale=SCALE,
                          bias=att[:, p, 4 + 2 * qt + m:5 + 2 * qt + m],
                          accum_out=att[:, p, z:z + 1]).then_inc(exp_ok, 1)

            for t in range(TICKS):
                g = t - 1
                if 0 < t < NH:
                    exponentials(t)
                for i, piece in enumerate(tick_chunks[t]):
                    if t == 0:
                        for c in (2 * i, 2 * i + 1):
                            act_e.wait_ge(cen_ok, c + 1)
                            if c >= 2:
                                act_e.wait_ge(csq_used, c - 1)
                            A(squares[:, c % 2, :], yT[:, c, :], ACT.Square).then_inc(csq_ok, 1)
                        if i == 1:
                            exponentials(t)
                    if piece:
                        split(place(piece) + 2)
                        if piece[0] == "in":
                            evacuate(piece[1])
                    if 0 <= g < NH and i < 2:
                        act_e.wait_ge(t_ps, 2 * g + i + 1)
                        if g >= 1:
                            act_e.wait_ge(m_ps, m_no["o", g - 1] + 1)
                        nb = 2 - i
                        b0 = 3 * i
                        nc.scalar.copy(aT[:, b0:b0 + nb, :], bank[6][:, 0:nb * P].rearrange("p (b q) -> p b q", q=P))
                        nc.scalar.copy(aT[0:M, b0 + nb, :], bank[6][0:M, nb * P:(nb + 1) * P]).then_inc(t_ok, 1)
                    if t == 1 and i == 1:
                        for c in range(KC):
                            act_e.wait_ge(z_ok, c + 1)
                            A(yT[:, c, :], yT[:, c, :], ACT.Silu, scale=cols[:, R_LNG + c:R_LNG + c + 1],
                              bias=cols[:, R_LNB + c:R_LNB + c + 1]).then_inc(y_ok, 1)
                    if t == 2 and i == 1:
                        for c in range(KC):
                            act_e.wait_ge(y_ok, c + 1)
                            nc.scalar.copy(yh[:, c, :], yT[:, c, :]).then_inc(yh_ok, 1)
                if 0 <= g < NH:
                    act_e.wait_ge(m_ok, m_no["o", g] + 1)
                    for qt in range(2):
                        A(junk[:, qt, :], o_sb[:, g % 4, qt, :], ACT.Square,
                          accum_out=osq[:, 0, g % 4, qt:qt + 1]).then_inc(osq_ok, 1)
                    if g % 4 == 3:
                        act_e.wait_ge(ovar_ok, g // 4 + 1)
                        A(osq[:, 2, :, :], osq[:, 1, :, :], ACT.Sqrt).then_inc(ostd_ok, 1)
                if t == 0:
                    act_e.wait_ge(cvar_ok, 1)
                    A(std, std, ACT.Sqrt).then_inc(cstd_ok, 1)
            for piece in tail_chunks:
                split(place(piece) + 2)
            act_e.wait_ge(m_ok, len(m_seq))
            for n in range(KC):
                c = SPLIT * 4 - KC + 2 + n
                if c < SPLIT * 4:
                    split(c)
                act_e.wait_ge(loaded[trunk_slot(SPLIT + n // 4)], 16 * load_no(SPLIT + n // 4))
                nc.scalar.copy(woh[:, n, :], w_out_rows(n)).then_inc(woh_ok, 1)
                act_e.wait_ge(mixed_ok, n + 1)
                nc.scalar.copy(mh[:, n, :], gaT[:, n, :]).then_inc(mh_ok, 1)

            for t in range(TT):
                act_e.wait_ge(h_ok, 2 * (t + 1))
                A(hn[:, t, :], h[:, t, :], ACT.Square, accum_out=st[:, 12 + t:13 + t]).then_inc(hsq_ok, 1)
                act_e.wait_ge(hvar_ok, t + 1)
                A(st[:, 14 + t:15 + t], st[:, 12 + t:13 + t], ACT.Sqrt).then_inc(hstd_ok, 1)
                act_e.wait_ge(hn_ok, t + 1)
                if t == 1:
                    act_e.wait_ge(out_ps, 2 * TT)
                nc.scalar.copy(parts[t][0], hn[:, t, :]).then_inc(part0_ok, 1)
            for t in range(TT):
                act_e.wait_ge(topn_ok, t + 1)
                A(rt[:, t, 4:8], top8[:, t, 0:TOP_K], ACT.Exp, bias=rt[:, t, 0:1],
                  accum_out=rt[:, t, 8:9]).then_inc(tope_ok, 1)

            def prepared(k, par):
                act_e.wait_ge(gather_ps, k + 1)
                nc.scalar.copy(xg[par], bank[4][:, :].rearrange("p (c s) -> p c s", s=SLOT)).then_inc(xg_ok, 1)
                act_e.wait_ge(scatT_ps, k + 1)
                nc.scalar.copy(scat[par], bank[7][:, 0:T]).then_inc(scatT_ok, 1)

            def expert(g, m, n, k):
                act_e.wait_ge(sig_in, n + 1)
                A(sig, glu_c, ACT.Sigmoid, scale=ALPHA).then_inc(sig_ok, 1)
                act_e.wait_ge(actT_ps, n + 1)
                nc.scalar.copy(actT, bank[7][:, :].rearrange("p (b z s) -> p b z s", z=2, s=SLOT)).then_inc(actT_ok, 1)
                act_e.wait_ge(*y_done(g, m))
                act_e.wait_ge(scat_done, n + 1)
                nc.scalar.copy(y_sb, bank[6][:, :]).then_inc(ysb_ok, 1)
                prepared(k, 1 - m % 2)

            prepared(0, 0)
            with act_e.Fori(0, GROUPS) as i:
                for m in range(UNROLL):
                    expert(i, m, i * UNROLL + m, i * UNROLL + (m + 1))
            act_e.wait_ge(rounds_ok, 1)
            n_rounds = act_e.value_load(flag[0:1, 0:1], min_val=1, max_val=T // SLOT)
            with act_e.If(n_rounds > 1):
                with act_e.Fori(1, n_rounds) as r:
                    prepared(r * GP, 0)
                    with act_e.Fori(0, GROUPS) as i:
                        for m in range(UNROLL):
                            expert(r * GROUPS + i, m, r * E + i * UNROLL + m, r * GP + i * UNROLL + (m + 1))
            with act_e.Else():
                act_e.nop()
            A(st[:, 26:27], st[:, 27:28], ACT.Sqrt)
            for t in range(TT):
                act_e.wait_ge(h2_ok, 2 * (t + 1))
                A(fin[:, t, :], h[:, t, :], ACT.Square, accum_out=st[:, 20 + t:21 + t]).then_inc(fsq_ok, 1)
                act_e.wait_ge(fvar_ok, t + 1)
                A(st[:, 22 + t:23 + t], st[:, 20 + t:21 + t], ACT.Sqrt).then_inc(fstd_ok, 1)

        @block.vector
        def _(ve):
            dv = nc.vector
            made = [0]

            def step(ins):
                ins.then_inc(dve, 1)
                made[0] += 1

            def settle(behind=0):
                ve.wait_ge(dve, made[0] - behind)

            dv.memset(st[:], 0.0).then_inc(zero_ok, 1)
            dv.memset(u[:, :, 0:PAD], 0.0)
            ve.wait_ge(const_ok, CONSTS)
            step(dv.scalar_tensor_tensor(dist[:], dist[:], -1.0, dist[:], ALU.mult, ALU.max))
            settle()
            step(dv.memset(dist[0:CHUNK, M + CHUNK:M + P], FAR))
            step(dv.memset(dist[0:CHUNK, SW - CHUNK:SW], FAR))

            ve.wait_ge(vec_ps, 1)
            dv.tensor_copy(cols[:, 0:ROWS], bank[7][:, 0:ROWS])
            dv.tensor_scalar(cols[:, ROWS:ROWS + 1], bank[7][:, R_SUB:R_SUB + 1], 1.0 - LAM_INIT, None, ALU.mult)
            dv.tensor_copy(taps[:], bank[7][:, P:P + TAPS * KC]).then_inc(vec_ok, 1)

            ve.wait_ge(sq_ok, 3)
            dv.tensor_scalar(st[:, 0:3], st[:, 0:3], 1.0 / D, EPS, ALU.mult, ALU.add).then_inc(var_ok, 1)
            ve.wait_ge(rs_ok, 1)
            step(dv.reciprocal(st[:, 3:6], st[:, 3:6]))
            settle()
            for t in range(3):
                n = P if t < 2 else M
                src = h[:, t, :] if t < 2 else h_meta[0:M, :]
                dv.tensor_scalar(h_norm[0:n, t, :], src, st[0:n, 3 + t:4 + t], None, ALU.mult).then_inc(hs_ok, 1)
            for c in range(KC):
                ve.wait_ge(xT_ps, c + 1)
                if c < XH_DVE:
                    dv.tensor_scalar(xh[:, c, :], bank[c][:, 0:L], cols[:, R_MIX + c:R_MIX + c + 1], None,
                                    ALU.mult).then_inc(xh_dve, 1)
                    ve.wait_ge(xh_dve, c + 1)
                else:
                    ve.wait_ge(xh_ok, c - XH_DVE + 1)
                dv.scalar_tensor_tensor(xl[:, c, :], bank[c][:, 0:L], cols[:, R_MIX + c:R_MIX + c + 1],
                                       xh[:, c, :].bitcast(F32), ALU.mult, ALU.subtract).then_inc(xT_ok, 1)

            ve.wait_ge(lam_ld, 16)
            prod = junk[:, :, 0:HD]
            step(dv.tensor_tensor(prod, lam_in[:, 0:4:2, :], lam_in[:, 1:4:2, :], ALU.mult))
            settle()
            dv.reduce_sum(st[:, 6:8], prod, AX_X).then_inc(lam_arg, 1)

            for c0 in range(0, KC, 2):
                pair = (c0, c0 + 1)
                for c in pair:
                    ve.wait_ge(proj_ok, (c // 4) * 8 + 4 + c % 4 + 1)
                    step(dv.tensor_tensor(u[:, c, PAD:PAD + L], u[:, c, PAD:PAD + L], cbT[:, c, :], ALU.mult))
                for c in pair:
                    settle(1)
                    step(dv.tensor_scalar(yT[:, c, :], u[:, c, 0:T], taps[:, c:c + 1],
                                         cols[:, R_DWB + c:R_DWB + c + 1], ALU.mult, ALU.add))
                for k in range(1, TAPS):
                    for c in pair:
                        settle(1)
                        step(dv.scalar_tensor_tensor(yT[:, c, :], u[:, c, k:k + T],
                                                    taps[:, k * KC + c:k * KC + c + 1], yT[:, c, :],
                                                    ALU.mult, ALU.add))
                settle()
                dv.tensor_copy(att[:, 0, 0:1], st[:, 0:1]).then_inc(conv_ok, 2)
            ve.wait_ge(mean_ps, 1)
            step(dv.tensor_scalar(mean, bank[6][:, 0:T], 1.0 / D, None, ALU.mult))
            settle()
            for c in range(KC):
                dv.tensor_tensor(yT[:, c, :], yT[:, c, :], mean, ALU.subtract).then_inc(cen_ok, 1)
            def mix_conv(piece):
                n = piece[1]
                ve.wait_ge(proj_ps, IN_SLOTS * 4 + n + 1)
                dv.tensor_tensor(gcT[:, n, :], gcT[:, n, :], bank[n % 4][:, 0:T], ALU.mult).then_inc(mix_ok, 1)

            def normalise_outputs(half):
                ve.wait_ge(ostd_ok, half + 1)
                step(dv.reciprocal(osq[:, 1, :, :], osq[:, 2, :, :]))
                settle()
                for f in range(4):
                    for qt in range(2):
                        last = dv.tensor_scalar(o_sb[:, f, qt, :], o_sb[:, f, qt, :], osq[:, 1, f, qt:qt + 1],
                                               None, ALU.mult)
                    if f % 2:
                        last.then_inc(on_ok, 1)

            def turned(f):
                ve.wait_ge(m_ps, m_no["n", f] + 1)
                if f == 0:
                    ve.wait_ge(yl_ok, KC)
                src = bank[7][:, :].rearrange("p (f t) -> p f t", f=2)
                gain = cols[:, ROWS:ROWS + 1]
                dv.tensor_scalar(oh[:, 2 * f:2 * f + 2, :], src, gain, None, ALU.mult).then_inc(oh_ok, 1)
                ve.wait_ge(oh_ok, f + 1)
                dv.scalar_tensor_tensor(ol[:, 2 * f:2 * f + 2, :], src, gain, oh[:, 2 * f:2 * f + 2, :].bitcast(F32),
                                       ALU.mult, ALU.subtract).then_inc(m_ok, 1)

            spans = ((0, M + P), (M + P, SW))
            for t in range(TICKS):
                g = t - 1
                pieces = [p if p and p[0] == "conv" else None for p in tick_chunks[t]]
                if t < NH:
                    p = t % 2
                    slope = 2.0 ** (-8.0 * (t + 1) / NH)
                    ve.wait_ge(score_done, t + 1)
                    dv.scalar_tensor_tensor(s_sb[:, p, :, :], dist[:].unsqueeze(1).broadcast_to([P, 2, SW]),
                                           -slope / SCALE, score_ps[:, :, 0:SW], ALU.mult, ALU.add).then_inc(score_read, 1)
                    ve.wait_ge(score_read, t + 1)
                    for qt, (c0, c1) in enumerate(spans):
                        step(dv.reduce_max(att[:, p, 2 * qt:2 * qt + 2], s_sb[:, p, :, c0:c1], AX_X))
                    settle()
                    dv.tensor_scalar(att[:, p, 4:8], att[:, p, 0:4], -SCALE, None, ALU.mult).then_inc(negmax_ok, 1)
                    ve.wait_ge(m_ps, m_no["v", t] + 1)
                    dv.tensor_copy(v_tok[:, 0:2, t, :], bank[7][:, 0:2 * P].rearrange("p (b d) -> p b d", d=P))
                    dv.tensor_copy(v_tok[0:M, 2, t, :], bank[7][0:M, 2 * P:3 * P]).then_inc(m_ok, 1)
                if t == NH // 2 + 1:
                    normalise_outputs(0)
                for i in range(2):
                    if pieces[i]:
                        mix_conv(pieces[i])
                    if i < len(turns(t)):
                        turned(turns(t)[i])
                if t == 0:
                    ve.wait_ge(lam_exp, 1)
                    step(dv.tensor_tensor(st[:, 10:11], st[:, 9:10], st[:, 8:9], ALU.subtract))
                    settle()
                    step(dv.tensor_scalar(st[:, 11:12], st[:, 10:11], -LAM_INIT, None, ALU.add))
                if t == 1:
                    ve.wait_ge(cstd_ok, 1)
                    step(dv.reciprocal(std, std))
                    settle()
                    for c in range(KC):
                        dv.tensor_tensor(yT[:, c, :], yT[:, c, :], std, ALU.mult).then_inc(z_ok, 1)
                if t < NH:
                    ve.wait_ge(exp_ok, 4 * (t + 1))
                    step(dv.reciprocal(att[:, p, 12:16], att[:, p, 8:12]))
                    settle()
                    step(dv.tensor_scalar(att[:, p, 13:16:2], att[:, p, 13:16:2], st[:, 11:12], None, ALU.mult))
                    if t >= 1:
                        ve.wait_ge(t_ps, 2 * t)
                    for qt, (c0, c1) in enumerate(spans):
                        step(dv.tensor_scalar(a_sb[:, c0:c1], s_sb[:, p, 0, c0:c1], att[:, p, 12 + 2 * qt:13 + 2 * qt],
                                             None, ALU.mult))
                    for qt, (c0, c1) in enumerate(spans):
                        settle(1 - qt)
                        last = dv.scalar_tensor_tensor(a_sb[:, c0:c1], s_sb[:, p, 1, c0:c1],
                                                      att[:, p, 13 + 2 * qt:14 + 2 * qt], a_sb[:, c0:c1],
                                                      ALU.mult, ALU.add)
                    last.then_inc(a_ok, 1)
                if t == 0:
                    ve.wait_ge(cvar_ps, 1)
                    dv.tensor_scalar(std, bank[6][:, 0:T], 1.0 / D, EPS, ALU.mult, ALU.add).then_inc(cvar_ok, 1)
                if 0 <= g < NH:
                    ve.wait_ge(m_ps, m_no["o", g] + 1)
                    dv.tensor_copy(o_sb[:, g % 4, :, :], bank[7][:, 0:2 * P].rearrange("p (a d) -> p a d", d=P)).then_inc(m_ok, 1)
                    if g % 4 == 3:
                        ve.wait_ge(osq_ok, 2 * (g + 1))
                        dv.tensor_scalar(osq[:, 1, :, :], osq[:, 0, :, :], 1.0 / P, EPS, ALU.mult, ALU.add).then_inc(ovar_ok, 1)
                        if g == NH - 1:
                            normalise_outputs(1)
            for piece in tail_chunks:
                mix_conv(piece)
            turned(2)
            turned(3)
            def rests(n):
                ve.wait_ge(woh_ok, n + 1)
                dv.tensor_tensor(wol[n], w_out_rows(n), woh[:, n, :].bitcast(F32), ALU.subtract).then_inc(wol_ok, 1)
                ve.wait_ge(mh_ok, n + 1)
                dv.tensor_tensor(ml[:, n, :], gaT[:, n, :], mh[:, n, :].bitcast(F32), ALU.subtract).then_inc(ml_ok, 1)

            for n in range(KC):
                ve.wait_ge(proj_ps, IN_SLOTS * 4 + KC + n + 1)
                dv.tensor_tensor(gaT[:, n, :], gaT[:, n, :], bank[n % 4][:, 0:T], ALU.mult).then_inc(mix_ok, 1)
                ve.wait_ge(mix_ok, KC + n + 1)
                dv.tensor_tensor(gaT[:, n, :], gaT[:, n, :], gcT[:, n, :], ALU.add).then_inc(mixed_ok, 1)
                if n:
                    rests(n - 1)
            rests(KC - 1)

            def bias_round(r):
                dv.tensor_copy(bias_gu[r, :], bias_f32[r, :]).then_inc(bias_dve, 1)

            ve.wait_ge(bgu_in, 48)
            bias_round(slice(0, 3 * E))
            ve.wait_ge(gain_in, 16)
            for t in range(TT):
                for z in range(2):
                    b = 2 * t + z
                    ve.wait_ge(out_ps, b + 1)
                    dv.tensor_tensor(h[:, t, z * FH:(z + 1) * FH], h[:, t, z * FH:(z + 1) * FH], bank[b][:, :],
                                     ALU.add).then_inc(h_ok, 1)
                    if b == 0:
                        for q in (1, 2):
                            ve.wait_ge(off_ok, q)
                            bias_round(slice(q * E, (q + 1) * E))
                ve.wait_ge(hsq_ok, t + 1)
                dv.tensor_scalar(st[:, 12 + t:13 + t], st[:, 12 + t:13 + t], 1.0 / D, EPS, ALU.mult,
                                 ALU.add).then_inc(hvar_ok, 1)
                ve.wait_ge(hstd_ok, t + 1)
                step(dv.reciprocal(st[:, 16 + t:17 + t], st[:, 14 + t:15 + t]))
                settle()
                dv.scalar_tensor_tensor(hn[:, t, :], h[:, t, :], st[:, 16 + t:17 + t], gain_ffn,
                                        ALU.mult, ALU.mult).then_inc(hn_ok, 1)
                if t == 1:
                    dv.memset(slot[:, :, E:GP], -1.0)
                    dv.memset(gate[:, :, E:GP], 0.0)
                    dv.memset(scat[1], 0.0)
                    dv.memset(y_sb, 0.0).then_inc(ysb_ok, 1)
                for b in (2 * t, 2 * t + 1):
                    ve.wait_ge(hT_ps, b + 1)
                    dv.tensor_copy(hnT[:, t, 4 * (b % 2):4 * (b % 2) + 4, :],
                                   bank[4 + b][:, :].rearrange("p (c t) -> p c t", t=P)).then_inc(hT_ok, 1)
                if t == 0:
                    ve.wait_ge(part0_ok, 1)
                    step(dv.tensor_tensor(hn[:, 0, :], hn[:, 0, :], parts[0][0], ALU.subtract))
                    settle()
                    step(dv.tensor_copy(parts[0][1], hn[:, 0, :]))
            settle()
            dv.tensor_tensor(parts[0][2], hn[:, 0, :], parts[0][1], ALU.subtract).then_inc(part2_ok, 1)
            ve.wait_ge(off_ok, 3)
            bias_round(slice(2 * E, 3 * E))

            def build(k, par, e, first=False):
                if not first:
                    ve.wait_ge(scatT_ps, k)
                for t in range(TT):
                    dv.tensor_scalar(pick[:, t, :], iota2[:, 0, :], slot[:, t, bass.ds(e, 1)], None, ALU.is_equal)
                    dv.tensor_scalar(gpick[:, t, :, :], iota2[:], slot[:, t, bass.ds(e, 1)],
                                    gate[:, t, bass.ds(e, 1)], ALU.is_equal, ALU.mult)
                dv.tensor_copy(esel[par], eye3[0:3 * E, bass.ds(e, 1)].broadcast_to([3 * E, SLOT])).then_inc(pick_ok, 1)

            for t in range(TT):
                ve.wait_ge(lg_ps, t + 1)
                step(dv.tensor_tensor(logits[:, t, :], bank[4 + t][:, 0:E], br[:], ALU.add))
            for t in range(TT):
                settle(1)
                step(dv.max(top8[:, t, :], logits[:, t, :]))
            for t in range(TT):
                settle(1)
                step(dv.max_index(idx8[:, t, :], top8[:, t, :], logits[:, t, :]))
                dv.tensor_scalar(rt[:, t, 0:1], top8[:, t, 0:1], -1.0, None, ALU.mult).then_inc(topn_ok, 1)
            settle()
            step(dv.tensor_copy(idxf[:, :, :], idx8[:, :, :]))
            settle()
            table = [P, TT, TOP_K, E]
            step(dv.tensor_tensor(eqs, iota2[:, 0, 0:E].unsqueeze(1).unsqueeze(1).broadcast_to(table),
                                  idxf[:, :, 0:TOP_K].unsqueeze(3).broadcast_to(table), ALU.is_equal))
            for t in range(TT):
                ve.wait_ge(tope_ok, t + 1)
                step(dv.reciprocal(rt[:, t, 9:10], rt[:, t, 8:9]))
            for t in range(TT):
                settle(1)
                step(dv.tensor_scalar(rt[:, t, 12:16], rt[:, t, 4:8], rt[:, t, 9:10], None, ALU.mult))
            settle()
            step(dv.tensor_tensor(eqs, eqs, rt[:, :, 12:16].unsqueeze(3).broadcast_to(table), ALU.mult))
            settle()
            for t in range(TT):
                step(dv.tensor_reduce(gate[:, t, 0:E], eqs[:, t, :, :].rearrange("p j e -> p e j"), AX_X, ALU.add))
            settle()
            dv.tensor_scalar(member, gate[:, :, 0:E], 0.0, None, ALU.is_gt).then_inc(memb_ok, 1)
            ve.wait_ge(memb_ok, 1)
            ve.wait_ge(num_ps, 1)
            for t in range(TT):
                step(dv.scalar_tensor_tensor(slot[:, t, 0:E], bank[5][:, t * E:(t + 1) * E], 1.0,
                                            member[:, t, :], ALU.add, ALU.mult))
            settle()
            step(dv.tensor_scalar(slot[:, :, 0:E], slot[:, :, 0:E], -1.0, None, ALU.add))
            settle()
            build(0, 0, 0, first=True)
            ve.wait_ge(gT_ps, 1)
            dv.tensor_copy(gateT[0:E, :], bank[6][0:E, 0:T]).then_inc(gT_ok, 1)
            step(dv.reduce_max(counts[:, 0:1], bank[5][:, 2 * E:3 * E], AX_X))
            settle()
            step(dv.tensor_scalar(counts[:, 4:7], thr[:], counts[:, 0:1], None, ALU.is_lt))
            settle()
            step(dv.reduce_sum(counts[:, 8:9], counts[:, 4:7], AX_X))
            settle()
            step(dv.tensor_scalar(counts[:, 9:10], counts[:, 8:9], 1.0, None, ALU.add))
            settle()
            dv.tensor_copy(flag[:], counts[:, 9:10]).then_inc(rounds_ok, 1)
            def expert(g, m, n, k, e):
                build(k, 1 - m % 2, e + 1)
                ve.wait_ge(*gu_done(g, m))
                dv.tensor_scalar(glu_c, bank[4][:, :], LIMIT, None, ALU.min).then_inc(sig_in, 1)
                dv.tensor_scalar(lin_c, bank[5][:, :], LIMIT, -LIMIT, ALU.min, ALU.max).then_inc(gu_read, 1)
                ve.wait_ge(gu_read, n + 2)
                dv.scalar_tensor_tensor(lin_c, lin_c, 1.0, glu_c, ALU.add, ALU.mult).then_inc(lin_ok, 1)
                ve.wait_ge(lin_ok, n + 1)
                ve.wait_ge(sig_ok, n + 1)
                dv.tensor_tensor(act, lin_c, sig, ALU.mult).then_inc(act_ok, 1)

            settle()
            dv.memset(counts[:, 15:16], 0.0).then_inc(gu_read, 1)
            with ve.Fori(0, GROUPS) as i:
                for m in range(UNROLL):
                    expert(i, m, i * UNROLL + m, i * UNROLL + (m + 1), i * UNROLL + m)
            ve.wait_ge(rounds_ok, 1)
            n_rounds = ve.value_load(flag[0:1, 0:1], min_val=1, max_val=T // SLOT)
            with ve.If(n_rounds > 1):
                with ve.Fori(1, n_rounds) as r:
                    ve.wait_ge(pick_ok, r * GP)
                    dv.tensor_scalar(slot[:], slot[:], -float(SLOT), None, ALU.add).then_inc(shift_ok, 1)
                    ve.wait_ge(shift_ok, r)
                    build(r * GP, 0, 0)
                    with ve.Fori(0, GROUPS) as i:
                        for m in range(UNROLL):
                            expert(r * GROUPS + i, m, r * E + i * UNROLL + m, r * GP + i * UNROLL + (m + 1),
                                   i * UNROLL + m)
            with ve.Else():
                ve.nop()
            ve.wait_ge(gainf_in, 16)

            def residual(t):
                ve.wait_ge(acc_ok, t + 1)
                for z in range(2):
                    dv.tensor_tensor(h[:, t, z * FH:(z + 1) * FH], h[:, t, z * FH:(z + 1) * FH],
                                    bank[2 * t + z][:, :], ALU.add).then_inc(h2_ok, 1)

            residual(0)
            residual(1)
            for t in range(TT):
                ve.wait_ge(fsq_ok, t + 1)
                dv.tensor_scalar(st[:, 20 + t:21 + t], st[:, 20 + t:21 + t], 1.0 / D, EPS, ALU.mult, ALU.add).then_inc(fvar_ok, 1)
                ve.wait_ge(fstd_ok, t + 1)
                dv.reciprocal(st[:, 24 + t:25 + t], st[:, 22 + t:23 + t]).then_inc(frec_ok, 1)
                ve.wait_ge(frec_ok, t + 1)
                dv.scalar_tensor_tensor(fin[:, t, :], h[:, t, :], st[:, 24 + t:25 + t], gain_fin,
                                       ALU.mult, ALU.mult).then_inc(fin_ok, 1)

        @block.tensor
        def _(pe):
            MM, TR = nc.tensor.matmul, nc.tensor.transpose
            pe.wait_ge(const_ok, CONSTS)

            def keep_warm(n):
                for _ in range(n):
                    last = MM(bank[7][:, 0:P], ones_bf[:], ones_bf[:], start=True, stop=True)

            keep_warm(60)
            pe.wait_ge(vec_in, 16 * 6)
            pe.wait_ge(taps_in, 32)
            half = TAPS * KC // 2
            TR(bank[7][:, 0:ROWS], rows[0:ROWS, :], ident[0:ROWS, 0:ROWS])
            for a in range(2):
                last = TR(bank[7][:, P + a * half:P + (a + 1) * half], dw_rows[0:half, a, :], ident[0:half, 0:half])
            last.then_inc(vec_ps, 1)
            pe.wait_ge(vec_ok, 1)
            keep_warm(60)
            pe.wait_ge(hs_ok, 3)
            for c in range(KC):
                TR(bank[c][:, 0:M], h_norm[0:M, 2, c * P:(c + 1) * P], ident[0:M, 0:M])
                for t in range(TT):
                    last = TR(bank[c][:, M + t * P:M + (t + 1) * P], h_norm[:, t, c * P:(c + 1) * P], ident[:])
                last.then_inc(xT_ps, 1)

            def bank_free(c):
                if c < 4:
                    pe.wait_ge(xT_ok, c + 1)
                elif c - 4 < IN_SLOTS * 4:
                    pe.wait_ge(proj_ok, c - 3)
                else:
                    pe.wait_ge(mix_ok, c - 3 - IN_SLOTS * 4)

            def project(c, hi, lo, ready=None):
                w, dst = c % 2, bank[c % 4][:, 0:hi.shape[2]]
                bank_free(c)
                pe.wait_ge(wh_ok, c + 1)
                for k in range(KC):
                    if ready:
                        pe.wait_ge(*ready(k))
                    MM(dst, wh[w][:, k, :], hi[:, k, :], start=(k == 0), stop=False)
                    last = MM(dst, wh[w][:, k, :], lo[:, k, :], start=False, stop=False)
                last.then_inc(wh_used, 1)
                pe.wait_ge(wl_ok, c + 1)
                for k in range(KC):
                    last = MM(dst, wl[w][:, k, :], hi[:, k, :], start=False, stop=(k == KC - 1))
                last.then_inc(proj_ps, 1)

            def project_in(c):
                ready = (lambda k: (xT_ok, k + 1)) if c == 0 else None
                if ORDER[c // 4][0] in (Q, GA, GC):
                    project(c, xh[:, :, M:L], xl[:, :, M:L], ready)
                else:
                    project(c, xh, xl, ready)

            def project_conv(n):
                pe.wait_ge(yl_ok, KC)
                project(IN_SLOTS * 4 + n, yh, yl)

            for c in range(LATE0):
                project_in(c)
            for c in range(KC):
                pe.wait_ge(conv_ok, c + 1)
                last = MM(bank[6][:, 0:T], ones[:], yT[:, c, :], start=(c == 0), stop=(c == KC - 1))
            last.then_inc(mean_ps, 1)
            def m_free(key):
                if m_no[key] > 0:
                    pe.wait_ge(m_ok, m_no[key])

            def turn(f):
                m_free(("n", f))
                pe.wait_ge(on_ok, f + 1)
                for j in range(4):
                    last = TR(bank[7][:, j * P:(j + 1) * P], o_sb[:, (2 * f + j // 2) % 4, j % 2, :], ident[:])
                last.then_inc(m_ps, 1)

            def scores(t):
                pe.wait_ge(proj_ok, run_chunk(K_, t) + 1)
                if t >= 1:
                    pe.wait_ge(score_read, t)
                for qt in range(2):
                    c0, n = (0, M + P) if qt == 0 else (M + P, L)
                    for m in range(2):
                        last = MM(score_ps[:, m, c0:c0 + n], qT[m * HD:(m + 1) * HD, t, qt * P:(qt + 1) * P],
                                  kT[m * HD:(m + 1) * HD, t, 0:n], start=True, stop=True)
                last.then_inc(score_done, 1)

            scores(0)
            for t in range(TICKS):
                g = t - 1
                if t < NH:
                    m_free(("v", t))
                    pe.wait_ge(proj_ok, run_chunk(V, t) + 1)
                    for b in range(2):
                        TR(bank[7][:, b * P:(b + 1) * P], vT[:, t, M + b * P:M + (b + 1) * P], ident[:])
                    TR(bank[7][0:M, 2 * P:3 * P], vT[:, t, 0:M], ident[:]).then_inc(m_ps, 1)
                for i, piece in enumerate(tick_chunks[t]):
                    if piece:
                        (project_in if piece[0] == "in" else project_conv)(piece[1])
                    if t == 0:
                        for c in (2 * i, 2 * i + 1):
                            pe.wait_ge(csq_ok, c + 1)
                            MM(bank[6][:, 0:T], ones[:], squares[:, c % 2, :], start=(c == 0),
                               stop=(c == KC - 1)).then_inc(cvar_ps if c == KC - 1 else csq_used, 1)
                    if 0 <= g < NH and i < 2:
                        if i == 0:
                            pe.wait_ge(a_ok, g + 1)
                        if 2 * g + i > 0:
                            pe.wait_ge(t_ok, 2 * g + i)
                        else:
                            pe.wait_ge(cvar_ok, 1)
                        c0 = M + P if i == 0 else 0
                        for b in range(2 - i):
                            TR(bank[6][:, b * P:(b + 1) * P], a_sb[:, c0 + M + b * P:c0 + M + (b + 1) * P], ident[:])
                        b = 2 - i
                        TR(bank[6][0:M, b * P:(b + 1) * P], a_sb[:, c0:c0 + M], ident[:]).then_inc(t_ps, 1)
                    if i < len(turns(t)):
                        turn(turns(t)[i])
                if t + 1 < NH:
                    scores(t + 1)
                if 0 <= g < NH:
                    m_free(("o", g))
                    pe.wait_ge(t_ok, 2 * g + 2)
                    for qt, blocks in ((0, ((3, 0), (4, 2))), (1, ((0, 0), (1, 1), (2, 2)))):
                        for i, (b, vb) in enumerate(blocks):
                            n = M if vb == 2 else P
                            last = MM(bank[7][:, qt * P:(qt + 1) * P], aT[0:n, b, :], v_tok[0:n, vb, g, :],
                                      start=(i == 0), stop=(i == len(blocks) - 1))
                    last.then_inc(m_ps, 1)
            for piece in tail_chunks:
                project_conv(piece[1])
            turn(2)
            turn(3)
            for n in range(KC):
                project(IN_SLOTS * 4 + KC + n, oh, ol,
                        (lambda k: (m_ok, m_no["n", k // 2] + 1)) if n == 0 else None)
            def out_project(b):
                t, z = divmod(b, 2)
                pe.wait_ge(mix_ok, KC + 4 + b + 1)
                tile, half = slice(t * P, (t + 1) * P), slice(z * FH, (z + 1) * FH)
                for k in range(KC):
                    if b == 0:
                        pe.wait_ge(ml_ok, k + 1)
                        pe.wait_ge(woh_ok, k + 1)
                    MM(bank[b][:, :], mh[:, k, tile], woh[:, k, half], start=(k == 0), stop=False)
                    MM(bank[b][:, :], ml[:, k, tile], woh[:, k, half], start=False, stop=False)
                for k in range(KC):
                    if b == 0:
                        pe.wait_ge(wol_ok, k + 1)
                    last = MM(bank[b][:, :], mh[:, k, tile], wol[k][:, half], start=False, stop=(k == KC - 1))
                last.then_inc(out_ps, 1)

            def turn_tokens(t):
                pe.wait_ge(hn_ok, t + 1)
                for c in range(KC):
                    last = TR(bank[4 + 2 * t + c // 4][:, (c % 4) * P:(c % 4 + 1) * P], hn[:, t, c * P:(c + 1) * P], ident[:])
                    if c % 4 == 3:
                        last.then_inc(hT_ps, 1)

            def logit_products(t):
                pe.wait_ge(hT_ok, 2 * t + 2)
                pe.wait_ge(small_in, 32)
                for c in range(KC):
                    last = MM(bank[4 + t][:, 0:E], hnT[:, t, c, :], wr[:, c, :], start=(c == 0), stop=(c == KC - 1))
                last.then_inc(lg_ps, 1)

            out_project(0)
            out_project(1)
            out_project(2)
            turn_tokens(0)
            out_project(3)
            logit_products(0)
            turn_tokens(1)
            logit_products(1)
            pe.wait_ge(hT_ok, 4)
            keep_warm(36)
            pe.wait_ge(memb_ok, 1)
            MM(bank[5][:, 0:E], before[:], member[:, 0, :], start=True, stop=True)
            MM(bank[5][:, E:2 * E], ones_bf[:], member[:, 0, :], start=True, stop=False)
            MM(bank[5][:, E:2 * E], before[:], member[:, 1, :], start=False, stop=True)
            MM(bank[5][:, 2 * E:3 * E], ones_bf[:], member[:, 0, :], start=True, stop=False)
            MM(bank[5][:, 2 * E:3 * E], ones_bf[:], member[:, 1, :], start=False, stop=True).then_inc(num_ps, 1)
            for t in range(TT):
                last = TR(bank[6][0:E, t * P:(t + 1) * P], gate[:, t, 0:E], ident[:])
            last.then_inc(gT_ps, 1)
            keep_warm(10)

            def prepare(k):
                pe.wait_ge(pick_ok, k + 1)
                for c in range(KC):
                    for i in range(3 * TT):
                        last = MM(bank[4][:, c * SLOT:(c + 1) * SLOT], parts[i % TT][i // TT][:, c * P:(c + 1) * P],
                                  pick[:, i % TT, :], start=(i == 0), stop=(i == 3 * TT - 1))
                last.then_inc(gather_ps, 1)
                for t in range(TT):
                    last = TR(bank[7][:, t * P:(t + 1) * P], gpick[:, t, :, :].rearrange("p z s -> p (z s)"), ident[:])
                last.then_inc(scatT_ps, 1)

            def scatter(n, par, tile_done=None):
                pe.wait_ge(ysb_ok, n + 1)
                for t in range(TT):
                    for z in range(2):
                        last = MM(bank[2 * t + z][:, :], scat[par][z * SLOT:(z + 1) * SLOT, t * P:(t + 1) * P],
                                  y_sb[z * SLOT:(z + 1) * SLOT, :], start=False, stop=True, skip_group_check=True)
                    if tile_done:
                        last.then_inc(tile_done, 1)
                if not tile_done:
                    last.then_inc(scat_done, 1)

            def expert(g, m, n, k):
                par = m % 2
                pe.wait_ge(xg_ok, k)
                pe.wait_ge(gu_read, n + 1)
                for b in range(2):
                    for z in range(2):
                        q = 2 * b + z
                        MM(bank[4 + b][z * SLOT:(z + 1) * SLOT, :], esel[par], bias_gu[:, q * FH:(q + 1) * FH],
                           start=True, stop=False)
                for j in range(4):
                    s = moe_slot(m, j)
                    pe.wait_ge(loaded[s], (moe_turn(g, m, j) + (uses(s) + 1)) * 16)
                    w = ring[:, s, :].rearrange("p (k n) -> p k n", k=2)
                    for kk in range(2):
                        c = 2 * j + kk
                        for b in range(2):
                            for z in range(2):
                                q = 2 * b + z
                                last = MM(bank[4 + b][z * SLOT:(z + 1) * SLOT, :], xg[par][:, c, :],
                                          w[:, kk, q * FH:(q + 1) * FH], start=False, stop=(c == KC - 1))
                    last.then_inc(freed[s], 1)
                pe.wait_ge(scatT_ok, k)
                scatter(n, 1 - par)
                pe.wait_ge(act_ok, n + 1)
                for b in range(4):
                    last = TR(bank[7][:, b * P:(b + 1) * P], act[:, b * P:(b + 1) * P], ident[:])
                last.then_inc(actT_ps, 1)
                pe.wait_ge(actT_ok, n + 1)
                for j in range(4, 6):
                    s = moe_slot(m, j)
                    pe.wait_ge(loaded[s], (moe_turn(g, m, j) + (uses(s) + 1)) * 16)
                    w = ring[:, s, :].rearrange("p (k n) -> p k n", k=4)
                    for kk in range(4):
                        for z in range(2):
                            last = MM(bank[6][z * SLOT:(z + 1) * SLOT, :], actT[:, kk, j - 4, :],
                                      w[:, kk, z * FH:(z + 1) * FH], start=(j == 4 and kk == 0), stop=(j == 5 and kk == 3))
                    last.then_inc(freed[s], 1)
                prepare(k)

            pe.wait_ge(part2_ok, TT)
            prepare(0)
            pe.wait_ge(gT_ok, 1)
            pe.wait_ge(bdn_in, 16)
            for t in range(TT):
                for z in range(2):
                    MM(bank[2 * t + z][:, :], gateT[0:E, t * P:(t + 1) * P], bias_dn[0:E, z * FH:(z + 1) * FH],
                       start=True, stop=True)
            pe.wait_ge(bias_dve, 4)
            with pe.Fori(0, GROUPS) as i:
                for m in range(UNROLL):
                    expert(i, m, i * UNROLL + m, i * UNROLL + (m + 1))
            pe.wait_ge(rounds_ok, 1)
            n_rounds = pe.value_load(flag[0:1, 0:1], min_val=1, max_val=T // SLOT)
            with pe.If(n_rounds > 1):
                with pe.Fori(1, n_rounds) as r:
                    pe.wait_ge(xg_ok, r * GP)
                    pe.wait_ge(scatT_ok, r * GP)
                    prepare(r * GP)
                    with pe.Fori(0, GROUPS) as i:
                        for m in range(UNROLL):
                            expert(r * GROUPS + i, m, r * E + i * UNROLL + m, r * GP + i * UNROLL + (m + 1))
            with pe.Else():
                pe.nop()
            scatter(n_rounds * E, 1, tile_done=acc_ok)


_INS = ["x", "meta_tokens", "norm_mix", "w_in", "b_in", "lam_params", "subln_gain", "w_attn_proj",
        "conv_dw_w", "conv_dw_b", "conv_ln_g", "conv_ln_b", "w_conv_proj", "w_out", "norm_ffn",
        "w_router", "b_router", "w_gate_up", "b_gate_up", "w_down", "b_down", "norm_final"]


def kernel(**inputs):
    import concourse.bacc as bacc
    import numpy as np
    from concourse.bass_utils import run_bass_kernel_spmd

    nc = bacc.Bacc("TRN2", target_bir_lowering=False, num_devices=1)
    arrays, args = {}, []
    for name in _INS:
        a = np.ascontiguousarray(inputs[name])
        arrays[f"in_{name}"] = a
        args.append(nc.dram_tensor(f"in_{name}", a.shape, F32, kind="ExternalInput").ap())
    args.append(nc.dram_tensor("out", inputs["x"].shape, F32, kind="ExternalOutput").ap())
    encoder_block(nc, *args)
    r = run_bass_kernel_spmd(nc, [arrays], core_ids=[0])
    return r.results[0]["out"]
```
